# Optimizing a Trainium2 kernel written in Bass

```python
import math
import jax, jax.numpy as jnp
from jax import lax
import numpy as np

D_MODEL = 1024
BATCH = 1
SEQ = 256
DEPTH = 4

N_MIXERS = 3
Q_BLOCK = 128
RMS_EPS = 1e-6
SB_HEADS = 16
SB_HEAD_DIM = D_MODEL // SB_HEADS
S5_GROUP = 16
S5_GROUPS = D_MODEL // S5_GROUP
S5_STATE = 64
S5_DT_MIN = 1e-3
S5_DT_MAX = 1e-1
MLA_HEADS = 16
MLA_NOPE = 64
MLA_ROPE = 32
MLA_V = 64
MLA_Q_RANK = 384
MLA_KV_RANK = 256
ROPE_THETA = 10000.0
D_FF = 2816
N_EXPERTS = 8
TOP_K = 2
D_FF_EXPERT = 1408
N_SB = (DEPTH + 2) // 3
N_S5 = (DEPTH + 1) // 3
N_MLA = DEPTH // 3
N_DENSE = (DEPTH + 1) // 2
N_MOE = DEPTH // 2

kernel_name = 'hybrid_stickbreak_s5_mla_moe_trunk'

def rms_norm(x, g):
    xf = x.astype(jnp.float32)
    y = xf * lax.rsqrt(jnp.mean(xf * xf, axis=-1, keepdims=True) + RMS_EPS)
    return (y * g.astype(jnp.float32)).astype(x.dtype)

def stick_breaking_attention(h, w_qkv, w_o):
    b, l, _ = h.shape
    qkv = (h @ w_qkv).reshape(b, l, 3, SB_HEADS, SB_HEAD_DIM)
    q, k, v = qkv[:, :, 0], qkv[:, :, 1], qkv[:, :, 2]
    scale = SB_HEAD_DIM ** -0.5
    outs = []
    for start in range(0, l, Q_BLOCK):
        end = start + Q_BLOCK
        z = jnp.einsum('bqhd,bkhd->bhqk', q[:, start:end], k[:, :end]).astype(jnp.float32) * scale
        strict = jnp.arange(end)[None, :] < jnp.arange(start, end)[:, None]
        log_one_minus = jnp.where(strict, jax.nn.log_sigmoid(-z), 0.0)
        tail = lax.cumsum(log_one_minus, axis=3, reverse=True) - log_one_minus
        weights = jnp.where(strict, jnp.exp(jax.nn.log_sigmoid(z) + tail), 0.0)
        outs.append(jnp.einsum('bhqk,bkhd->bqhd', weights.astype(v.dtype), v[:, :end]))
    o = jnp.concatenate(outs, axis=1).reshape(b, l, SB_HEADS * SB_HEAD_DIM)
    return o @ w_o

def _complex_affine_combine(prev, nxt):
    a1r, a1i, b1r, b1i = prev
    a2r, a2i, b2r, b2i = nxt
    ar = a2r * a1r - a2i * a1i
    ai = a2r * a1i + a2i * a1r
    br = a2r * b1r - a2i * b1i + b2r
    bi = a2r * b1i + a2i * b1r + b2i
    return (ar, ai, br, bi)

def s5_layer(h, lam_re, lam_im, log_dt, b_re, b_im, c_re, c_im, d_skip, w_glu):
    f32 = jnp.float32
    bsz, l, _ = h.shape
    lam_re = lam_re.astype(f32)
    lam_im = lam_im.astype(f32)
    dt = jnp.exp(log_dt.astype(f32))[:, None]
    mag = jnp.exp(lam_re * dt)
    ang = lam_im * dt
    a_re, a_im = mag * jnp.cos(ang), mag * jnp.sin(ang)
    den = lam_re * lam_re + lam_im * lam_im
    num_re = a_re - 1.0
    f_re = (num_re * lam_re + a_im * lam_im) / den
    f_im = (a_im * lam_re - num_re * lam_im) / den
    b_re = b_re.astype(f32)
    b_im = b_im.astype(f32)
    bb_re = f_re[..., None] * b_re - f_im[..., None] * b_im
    bb_im = f_re[..., None] * b_im + f_im[..., None] * b_re
    u = h.reshape(bsz, l, S5_GROUPS, S5_GROUP).astype(f32)
    bu_re = jnp.einsum('blgc,gpc->lbgp', u, bb_re)
    bu_im = jnp.einsum('blgc,gpc->lbgp', u, bb_im)
    a_re_t = jnp.broadcast_to(a_re, (l, 1) + a_re.shape)
    a_im_t = jnp.broadcast_to(a_im, (l, 1) + a_im.shape)
    _, _, x_re, x_im = lax.associative_scan(_complex_affine_combine, (a_re_t, a_im_t, bu_re, bu_im), axis=0)
    y = (jnp.einsum('lbgp,gcp->blgc', x_re, c_re.astype(f32))
         - jnp.einsum('lbgp,gcp->blgc', x_im, c_im.astype(f32)))
    y = y.reshape(bsz, l, D_MODEL) + d_skip.astype(f32) * h.astype(f32)
    y = jax.nn.gelu(y).astype(h.dtype)
    val, gate = jnp.split(y @ w_glu, 2, axis=-1)
    return val * jax.nn.sigmoid(gate)

def apply_rope(t, cos, sin):
    half = t.shape[-1] // 2
    t1 = t[..., :half].astype(jnp.float32)
    t2 = t[..., half:].astype(jnp.float32)
    return jnp.concatenate([t1 * cos - t2 * sin, t1 * sin + t2 * cos], axis=-1).astype(t.dtype)

def mla_attention(h, w_in, q_norm, w_q_b, kv_norm, w_kv_b, w_o, cos, sin):
    b, l, _ = h.shape
    c = h @ w_in
    q_c = c[..., :MLA_Q_RANK]
    kv_c = c[..., MLA_Q_RANK:MLA_Q_RANK + MLA_KV_RANK]
    k_rope = apply_rope(c[..., MLA_Q_RANK + MLA_KV_RANK:], cos, sin)
    q = (rms_norm(q_c, q_norm) @ w_q_b).reshape(b, l, MLA_HEADS, MLA_NOPE + MLA_ROPE)
    q_nope = q[..., :MLA_NOPE]
    q_rope = apply_rope(q[..., MLA_NOPE:], cos[:, None, :], sin[:, None, :])
    kv = (rms_norm(kv_c, kv_norm) @ w_kv_b).reshape(b, l, MLA_HEADS, MLA_NOPE + MLA_V)
    k_nope, v = kv[..., :MLA_NOPE], kv[..., MLA_NOPE:]
    scale = (MLA_NOPE + MLA_ROPE) ** -0.5
    outs = []
    for start in range(0, l, Q_BLOCK):
        end = start + Q_BLOCK
        s = (jnp.einsum('bqhd,bkhd->bhqk', q_nope[:, start:end], k_nope[:, :end])
             + jnp.einsum('bqhr,bkr->bhqk', q_rope[:, start:end], k_rope[:, :end])).astype(jnp.float32) * scale
        causal = jnp.arange(end)[None, :] <= jnp.arange(start, end)[:, None]
        p = jax.nn.softmax(jnp.where(causal, s, -jnp.inf), axis=-1)
        outs.append(jnp.einsum('bhqk,bkhv->bqhv', p.astype(v.dtype), v[:, :end]))
    o = jnp.concatenate(outs, axis=1).reshape(b, l, MLA_HEADS * MLA_V)
    return o @ w_o

def swiglu(h, w_gate_up, w_down):
    g, u = jnp.split(h @ w_gate_up, 2, axis=-1)
    return (jax.nn.silu(g) * u) @ w_down

def moe_swiglu(h, w_router, b_router, w_gate_up, w_down):
    b, l, d = h.shape
    hf = h.reshape(b * l, d)
    logits = (hf @ w_router).astype(jnp.float32) + b_router.astype(jnp.float32)
    top_v, top_i = lax.top_k(logits, TOP_K)
    top_w = jax.nn.softmax(top_v, axis=-1)
    gates = jnp.sum(jax.nn.one_hot(top_i, N_EXPERTS, dtype=jnp.float32) * top_w[..., None], axis=1)
    out = jnp.zeros((b * l, d), jnp.float32)
    for e in range(N_EXPERTS):
        out = out + gates[:, e:e + 1] * swiglu(hf, w_gate_up[e], w_down[e]).astype(jnp.float32)
    return out.astype(h.dtype).reshape(b, l, d)

def setup_inputs(seed: int = 0) -> dict:
    key = jax.random.key(seed)
    ks = iter(jax.random.split(key, 32))
    f32 = jnp.float32

    def nrm(shape, scale):
        return jax.random.normal(next(ks), shape, f32) * scale

    def gain(shape):
        return 1.0 + 0.05 * jax.random.normal(next(ks), shape, f32)

    state_idx = jnp.arange(S5_STATE, dtype=f32)
    return {
        'x': nrm((BATCH, SEQ, D_MODEL), 1.0),
        'norm_mix': gain((DEPTH, D_MODEL)),
        'norm_ffn': gain((DEPTH, D_MODEL)),
        'final_norm': gain((D_MODEL,)),
        'sb_w_qkv': nrm((N_SB, D_MODEL, 3 * D_MODEL), D_MODEL ** -0.5),
        'sb_w_o': nrm((N_SB, D_MODEL, D_MODEL), D_MODEL ** -0.5),
        's5_lambda_re': -0.5 + 0.01 * jax.random.normal(next(ks), (N_S5, S5_GROUPS, S5_STATE), f32),
        's5_lambda_im': math.pi * state_idx + 0.01 * jax.random.normal(next(ks), (N_S5, S5_GROUPS, S5_STATE), f32),
        's5_log_dt': jax.random.uniform(next(ks), (N_S5, S5_GROUPS), f32, math.log(S5_DT_MIN), math.log(S5_DT_MAX)),
        's5_b_re': nrm((N_S5, S5_GROUPS, S5_STATE, S5_GROUP), (2 * S5_GROUP) ** -0.5),
        's5_b_im': nrm((N_S5, S5_GROUPS, S5_STATE, S5_GROUP), (2 * S5_GROUP) ** -0.5),
        's5_c_re': nrm((N_S5, S5_GROUPS, S5_GROUP, S5_STATE), S5_STATE ** -0.5),
        's5_c_im': nrm((N_S5, S5_GROUPS, S5_GROUP, S5_STATE), S5_STATE ** -0.5),
        's5_d': nrm((N_S5, D_MODEL), 1.0),
        's5_w_glu': nrm((N_S5, D_MODEL, 2 * D_MODEL), D_MODEL ** -0.5),
        'mla_w_in': nrm((N_MLA, D_MODEL, MLA_Q_RANK + MLA_KV_RANK + MLA_ROPE), D_MODEL ** -0.5),
        'mla_q_norm': gain((N_MLA, MLA_Q_RANK)),
        'mla_w_q_b': nrm((N_MLA, MLA_Q_RANK, MLA_HEADS * (MLA_NOPE + MLA_ROPE)), MLA_Q_RANK ** -0.5),
        'mla_kv_norm': gain((N_MLA, MLA_KV_RANK)),
        'mla_w_kv_b': nrm((N_MLA, MLA_KV_RANK, MLA_HEADS * (MLA_NOPE + MLA_V)), MLA_KV_RANK ** -0.5),
        'mla_w_o': nrm((N_MLA, MLA_HEADS * MLA_V, D_MODEL), (MLA_HEADS * MLA_V) ** -0.5),
        'ffn_w_gate_up': nrm((N_DENSE, D_MODEL, 2 * D_FF), D_MODEL ** -0.5),
        'ffn_w_down': nrm((N_DENSE, D_FF, D_MODEL), D_FF ** -0.5),
        'moe_w_router': nrm((N_MOE, D_MODEL, N_EXPERTS), D_MODEL ** -0.5),
        'moe_b_router': nrm((N_MOE, N_EXPERTS), 0.01),
        'moe_w_gate_up': nrm((N_MOE, N_EXPERTS, D_MODEL, 2 * D_FF_EXPERT), D_MODEL ** -0.5),
        'moe_w_down': nrm((N_MOE, N_EXPERTS, D_FF_EXPERT, D_MODEL), D_FF_EXPERT ** -0.5),
    }

def reference(x, norm_mix, norm_ffn, final_norm, sb_w_qkv, sb_w_o,
              s5_lambda_re, s5_lambda_im, s5_log_dt, s5_b_re, s5_b_im, s5_c_re, s5_c_im, s5_d, s5_w_glu,
              mla_w_in, mla_q_norm, mla_w_q_b, mla_kv_norm, mla_w_kv_b, mla_w_o,
              ffn_w_gate_up, ffn_w_down, moe_w_router, moe_b_router, moe_w_gate_up, moe_w_down):
    l = x.shape[1]
    pos = jnp.arange(l, dtype=jnp.float32)
    inv_freq = ROPE_THETA ** (-jnp.arange(0, MLA_ROPE, 2, dtype=jnp.float32) / MLA_ROPE)
    ang = pos[:, None] * inv_freq[None, :]
    cos, sin = jnp.cos(ang), jnp.sin(ang)
    for i in range(DEPTH):
        h = rms_norm(x, norm_mix[i])
        kind, slot = i % N_MIXERS, i // N_MIXERS
        if kind == 0:
            m = stick_breaking_attention(h, sb_w_qkv[slot], sb_w_o[slot])
        elif kind == 1:
            m = s5_layer(h, s5_lambda_re[slot], s5_lambda_im[slot], s5_log_dt[slot], s5_b_re[slot], s5_b_im[slot],
                         s5_c_re[slot], s5_c_im[slot], s5_d[slot], s5_w_glu[slot])
        else:
            m = mla_attention(h, mla_w_in[slot], mla_q_norm[slot], mla_w_q_b[slot], mla_kv_norm[slot],
                              mla_w_kv_b[slot], mla_w_o[slot], cos, sin)
        x = x + m.astype(x.dtype)
        h = rms_norm(x, norm_ffn[i])
        if i % 2 == 0:
            f = swiglu(h, ffn_w_gate_up[i // 2], ffn_w_down[i // 2])
        else:
            f = moe_swiglu(h, moe_w_router[i // 2], moe_b_router[i // 2], moe_w_gate_up[i // 2], moe_w_down[i // 2])
        x = x + f.astype(x.dtype)
    return rms_norm(x, final_norm)


_drawn_inputs = setup_inputs


def setup_inputs(seed=0):
    import zlib

    import numpy as np

    out = dict(_drawn_inputs(seed))
    spreads = {}
    factors = {'s5_lambda_re': 8.0, 'mla_q_norm': 3.749}
    for name, (base, spread) in spreads.items():
        noise = np.random.default_rng([zlib.crc32(name.encode()), seed]).standard_normal(out[name].shape)
        drawn = base * np.exp(spread * noise) if base else spread * noise
        out[name] = __import__('jax').numpy.asarray(drawn.astype(out[name].dtype))
    for name, factor in factors.items():
        out[name] = (out[name] * factor).astype(out[name].dtype)
    return out
```

```python
from contextlib import ExitStack

import numpy as np

import concourse.bass as bass
from concourse import mybir

F32 = mybir.dt.float32
F32R = mybir.dt.float32r
U32 = mybir.dt.uint32
I32 = mybir.dt.int32
ALU = mybir.AluOpType
ACT = mybir.ActivationFunctionType
AX = mybir.AxisListType

P = 128
D = 1024
L = 256
TT = L // P
KC = D // P
EPS = 1e-6
HEADS, HD = 16, 64
PAIRS = HEADS // 2
NOPE, ROPE, MV = 64, 32, 64
QR, KVR = 384, 256
QH = NOPE + ROPE
MLA_SCALE = float(QH) ** -0.5
ST = 32
SG, SS = 16, 64
FF, FE, NE = 2816, 1408, 8
W = 384
SLOT = KC * W
RAW, SPL = 4, 3
NEG = -1.0e30
CAP = P

C_ID, C_TRI, C_ONE, C_CAUSAL, C_IOTA, C_LOWER, C_ONES, C_COS, C_SIN, C_POW = (
    0, 128, 256, 384, 512, 768, 896, 1024, 1056, 1088)
C_END = 1092
TWO_PI = 2.0 * np.pi
PI_A = 6.28125
PI_B = float(np.float32(np.round((TWO_PI - PI_A) * 2 ** 22) / 2 ** 22))
PI_C = float(TWO_PI - PI_A - PI_B)
PI_MAX = 3.1415925


def constants():
    c = np.zeros((P, C_END), np.float32)
    i = np.arange(P)
    c[:, C_ID:C_ID + P] = np.eye(P)
    c[:, C_TRI:C_TRI + P] = -(i[:, None] >= i[None, :]).astype(np.float32)
    c[:, C_ONE:C_ONE + P] = -1.0
    c[:, C_CAUSAL:C_CAUSAL + P] = np.where(i[None, :] <= i[:, None], 0.0, NEG)
    c[:, C_IOTA:C_IOTA + 2 * P] = np.arange(2 * P)[None, :]
    c[:, C_LOWER:C_LOWER + P] = (i[:, None] < i[None, :]).astype(np.float32)
    c[:, C_ONES:C_ONES + P] = 1.0
    half = ROPE // 2
    inv = np.float32(10000.0) ** (-np.arange(0, ROPE, 2, dtype=np.float32) / np.float32(ROPE))
    ang = np.arange(L, dtype=np.float32)[:, None] * inv.astype(np.float32)[None, :]
    for t in range(TT):
        c[:, C_COS + half * t:C_COS + half * (t + 1)] = np.cos(ang[t * P:(t + 1) * P])
        c[:, C_SIN + half * t:C_SIN + half * (t + 1)] = np.sin(ang[t * P:(t + 1) * P])
    c[:, C_POW] = -0.5
    c[:, C_POW + 1] = -1.0
    c[:, C_POW + 2] = np.pi / 2
    return c


def widths(total, w=W):
    return [(c, min(w, total - c)) for c in range(0, total, w)]


def ffn_order(n):
    order = []
    for j in range(n + 2):
        if j < n:
            order.append(("g", j))
        if j >= 2:
            order.append(("d", j - 2))
        if j < n:
            order.append(("u", j))
    return order


def hybrid_trunk(nc, consts, x_in, norm_mix, norm_ffn, final_norm, sb_w_qkv, sb_w_o, lam_re_in, lam_im_in,
                 log_dt_in, b_re_in, b_im_in, c_re_in, c_im_in, s5_d, s5_w_glu, mla_w_in, mla_q_norm,
                 mla_w_q_b, mla_kv_norm, mla_w_kv_b, mla_w_o, ffn_w_gate_up, ffn_w_down, w_router,
                 b_router, moe_w_gate_up, moe_w_down, out):
    pieces = []
    base = {}

    def rows(w, k):
        return w.rearrange("(k p) n -> p k n", k=k)

    def add_cols(w, k, cols):
        for c0, cw in cols:
            pieces.append((rows(w, k)[:, :, c0:c0 + cw], k, cw))

    def add_ffn(gu, down, half):
        cols = widths(half)
        for kind, j in ffn_order(len(cols)):
            c0, cw = cols[j]
            if kind == "d":
                src = down[c0:c0 + cw, :].rearrange("(k p) n -> p k n", p=P)
                pieces.append((src, cw // P, D))
            else:
                c0 += half if kind == "u" else 0
                pieces.append((rows(gu, KC)[:, :, c0:c0 + cw], KC, cw))

    def mark(name):
        base[name] = len(pieces)

    DCOLS = widths(D)
    GU_D, GU_E = widths(FF), widths(FE)
    MOE_PIECES = 3 * len(GU_E)
    assert MOE_PIECES % RAW == 0 and MOE_PIECES % SPL == 0

    def add_sb(a):
        mark(f"sb{a}")
        for s in range(3):
            add_cols(sb_w_qkv[a], KC, [(s * D + c, w) for c, w in DCOLS])
        add_cols(sb_w_o[a], KC, DCOLS)

    def add_dense(f):
        mark(f"dense{f}")
        add_ffn(ffn_w_gate_up[f], ffn_w_down[f], FF)

    def add_moe(m):
        mark(f"moe{m}")
        for e in range(NE):
            add_ffn(moe_w_gate_up[m, e], moe_w_down[m, e], FE)

    add_sb(0)
    add_dense(0)
    mark("s5")
    for c0, cw in DCOLS:
        add_cols(s5_w_glu[0], KC, [(c0, cw), (D + c0, cw)])
    add_moe(0)
    mark("mla")
    add_cols(mla_w_in[0], KC, [(0, QR), (QR, KVR + ROPE)])
    for half in range(2):
        add_cols(mla_w_q_b[0], QR // P, [(half * 768, 768)])
        add_cols(mla_w_kv_b[0], KVR // P, [(half * 1024, 1024)])
    add_cols(mla_w_o[0], KC, DCOLS)
    add_dense(1)
    add_sb(1)
    add_moe(1)
    NP = len(pieces)

    with ExitStack() as ctx:
        def sb(name, shape, dt=F32):
            return ctx.enter_context(nc.sbuf_tensor(name, shape, dt))

        sems = {}

        def sem(name):
            sems[name] = ctx.enter_context(nc.semaphore(name))
            return sems[name]

        PS = ctx.enter_context(nc.psum_tensor("PS", [P, 8, 512], F32))
        psf = PS[:].rearrange("p b n -> p (b n)")

        raw = [sb(f"raw{i}", [P, SLOT]) for i in range(RAW)]
        whi = [sb(f"whi{i}", [P, SLOT], F32R) for i in range(SPL)]
        wlo = [sb(f"wlo{i}", [P, SLOT], F32R) for i in range(SPL)]
        x = sb("x", [P, TT, D])
        hT_hi = sb("hT_hi", [P, KC, L], F32R)
        hT_lo = sb("hT_lo", [P, KC, L], F32R)
        gain = sb("gain", [P, D])
        cst = sb("cst", [P, C_END])
        stat = sb("stat", [P, 4, 4])
        s5_par = sb("s5_par", [P, 5, ST])
        pk = sb("pk", [P, 4, ST])
        dT = sb("dT", [P, KC])
        most = sb("most", [P, 2], I32)
        ident = cst[:, C_ID:C_ID + P]
        negtri = cst[:, C_TRI:C_TRI + P]
        negone = cst[:, C_ONE:C_ONE + P]
        causal = cst[:, C_CAUSAL:C_CAUSAL + P]
        lower = cst[:, C_LOWER:C_LOWER + P]
        ones = cst[:, C_ONES:C_ONES + P]

        def stage(*tensors):
            made = {}
            with ExitStack() as scope:
                for name, shape, dt in tensors:
                    made[name] = scope.enter_context(nc.sbuf_tensor(name, shape, dt))
            return made

        H = ("h", [P, TT, D], F32)
        att = stage(("qT", [P, PAIRS, L], F32), ("kT", [P, PAIRS, L], F32), ("vv", [P, TT, D], F32),
                    ("az0", [P, 2, 384], F32), ("az1", [P, 2, 384], F32),
                    ("sp0", [P, 2, 384], F32), ("sp1", [P, 2, 384], F32),
                    ("pw0", [P, 2, 384], F32), ("pw1", [P, 2, 384], F32))
        KB = 256
        ff = stage(("sg", [P, TT, W], F32), ("act", [P, TT, W], F32),
                   ("ahi0", [P, 3 * L], F32R), ("ahi1", [P, 3 * L], F32R),
                   ("alo0", [P, 3 * L], F32R), ("alo1", [P, 3 * L], F32R),
                   ("ta_c", [P, ST, 16], F32), ("ta_s", [P, ST, 16], F32),
                   ("tb_c", [P, ST, 16], F32), ("tb_s", [P, ST, 16], F32),
                   ("tg0", [P, 2, 2, L], F32), ("tg1", [P, 2, 2, L], F32),
                   ("tm0", [P, 2, L], F32), ("tm1", [P, 2, L], F32))
        setup = stage(("pad_setup", [P, 42 * KB], F32),
                      ("r_lr", [ST, P], F32), ("r_li", [ST, P], F32), ("r_ldt", [ST, 2], F32),
                      ("r_dt", [ST, 2], F32), ("r_w", [ST, 14, P], F32))
        s5p = stage(("pad_s5p", [P, 28 * KB], F32), ("bpad", [P, 2, ST, 2, SG], F32),
                    ("cnat", [P, 2, KC, P], F32), ("dnat", [KC, P], F32), ("bnat", [P, 2, ST, SG], F32))
        s5q = stage(("pad_s5q", [P, 18 * KB], F32), ("btmp", [P, 2, ST, SG], F32))
        s5m = stage(("m12", [P, 2, L], F32), ("m34", [P, 2, L], F32), ("vvv", [P, 2, L], F32),
                    ("zz", [P, 2, L], F32), ("hTf", [P, KC, L], F32), ("bbt", [P, KC, 2, P], F32),
                    ("ct", [P, KC, 3, P], F32), ("bu0", [P, 2, L], F32), ("bu1", [P, 2, L], F32),
                    ("bu2", [P, 2, L], F32), ("bu3", [P, 2, L], F32), ("zz1", [P, 2, L], F32), ("uu", [P, 4, L], F32),
                    ("yt", [P, 2, L], F32))
        s5g = stage(("pad_s5g", [P, 8 * KB], F32), ("sgl", [P, TT, W], F32), ("prod", [P, TT, W], F32))
        s5p["btmp"] = s5q["btmp"]
        mo = stage(H, ("hh", [P, TT, D], F32R), ("hl", [P, TT, D], F32R),
                   ("gt", [P, D], F32), ("msg", [P, W], F32), ("mact", [P, W], F32),
                   ("mhi0", [P, W], F32R), ("mhi1", [P, W], F32R),
                   ("mlo0", [P, W], F32R), ("mlo1", [P, W], F32R),
                   ("pick", [P, TT, P], F32R), ("put", [P, TT, P], F32R),
                   ("yhi", [P, D], F32R), ("ylo", [P, D], F32R),
                   ("wr", [P, KC, NE], F32), ("wrh", [P, KC, NE], F32R), ("wrl", [P, KC, NE], F32R),
                   ("lg", [P, TT, NE], F32), ("top", [P, TT, NE], F32), ("topi", [P, TT, NE], U32),
                   ("topf", [P, TT, NE], F32), ("oh", [P, TT, 2, NE], F32), ("sel", [P, TT, NE], F32),
                   ("gw", [P, TT, 4], F32), ("route", [P, NE, 3, TT], F32), ("rb", [P, NE], F32), ("cmx", [P, 1], F32), ("lgt", [NE, L], F32),
                   ("cur", [P, 2, TT], F32), ("curg", [P, TT], F32))
        h = mo["h"]
        ov = stage(("pad_ov", [P, 8 * KB], F32), ("oT", [P, KC, P], F32), ("owg", [P, KC, P], F32),
                   ("owu", [P, KC, P], F32), ("owd", [P, D], F32), ("osilu", [P, P], F32), ("oact", [P, P], F32),
                   ("oy", [P, D], F32), ("opick", [P, TT, P], F32), ("oput", [P, TT, P], F32))
        ml = stage(("cn", [P, TT, QR + KVR + ROPE], F32), ("pad_ml", [P, 11 * KB - TT * (QR + KVR + ROPE)], F32),
                   ("mg", [P, QR + KVR], F32), ("pad_ml2", [P, 5 * KB - QR - KVR], F32),
                   ("kTm", [QH, HEADS, L], F32), ("vm", [P, TT, D], F32),
                   ("qt", [P, TT, HEADS // 2 * QH], F32), ("rt", [P, 4 * TT * HEADS // 2 * 16], F32),
                   ("pad_ml3", [P, 3 * KB], F32), ("st", [P, 12], F32), ("nm", [P, 4, 2], F32), ("mx", [P, 4, 2], F32),
                   ("sm", [P, HEADS, 2], F32), ("ri", [P, 2, HEADS // 2], F32))
        mlb = stage(("qTm", [QH, HEADS, L], F32), ("pad_mlb", [P, 24 * KB], F32),
                    ("pb0", [P, 384], F32), ("pb1", [P, 384], F32), ("pb2", [P, 384], F32), ("pb3", [P, 384], F32),
                    ("pt0", [P, 384], F32), ("pt1", [P, 384], F32), ("ot", [P, TT, 512], F32))
        ml.update({k: v for k, v in mlb.items()})
        tabs = nc.dram_tensor("s5_tables", [ST, P, 2 * L], F32, kind="Internal").ap()

        raw_in = [sem(f"raw_in{i}") for i in range(RAW)]
        hi_done = sem("hi_done")
        lo_done = sem("lo_done")
        w_used = sem("w_used")
        x_in_s = [sem(f"x_in{t}") for t in range(TT)]
        cst_in = sem("cst_in")
        gain_in = sem("gain_in")
        x_up = sem("x_up")
        chain_v, chain_g = sem("chain_v"), sem("chain_g")
        nrm_sq, nrm_ms, nrm_rs, nrm_h = sem("nrm_sq"), sem("nrm_ms"), sem("nrm_rs"), sem("nrm_h")
        nrm_tp, nrm_hi, nrm_lo = sem("nrm_tp"), sem("nrm_hi"), sem("nrm_lo")
        out_s = sem("out_s")
        CHAIN_M = [0]

        def split3(pe, o, st, mv, start, stop):
            (sh, sl), (mh, mlw) = st, mv
            pe.matmul(o, sh, mlw, start=start, stop=False, skip_group_check=True)
            pe.matmul(o, sl, mh, start=False, stop=False, skip_group_check=True)
            return pe.matmul(o, sh, mh, start=False, stop=stop, skip_group_check=True)

        def wpiece(p, k, w):
            v = [q[p % SPL][:, 0:k * w].rearrange("p (k w) -> p k w", k=k) for q in (whi, wlo)]
            return v[0], v[1]

        def at(pair, *ix):
            return pair[0][ix], pair[1][ix]

        def psize(p0):
            return pieces[p0][1] * pieces[p0][2]

        def load_piece(sp, p0, src=None, de=0):
            if p0 >= RAW:
                sp.wait_ge(lo_done, p0 - RAW + 1 + MOE_PIECES * de)
            s, k, w = pieces[p0]
            s = s if src is None else src
            sp.dma_start(raw[p0 % RAW][:, 0:k * w].rearrange("p (k w) -> p k w", k=k), s)\
                .then_inc(raw_in[p0 % RAW], 16)

        def split_hi(act, p0, de=0):
            if p0 >= NP:
                return
            n = psize(p0)
            act.wait_ge(raw_in[p0 % RAW], 16 * (p0 // RAW + 1) + 16 * (MOE_PIECES // RAW) * de)
            if p0 >= SPL:
                act.wait_ge(w_used, p0 - SPL + 1 + MOE_PIECES * de)
            act.activation(whi[p0 % SPL][:, 0:n], raw[p0 % RAW][:, 0:n], ACT.Copy).then_inc(hi_done, 1)

        def split_lo(dve, p0, de=0):
            if p0 >= NP:
                return
            n = psize(p0)
            dve.wait_ge(hi_done, p0 + 1 + MOE_PIECES * de)
            dve.tensor_tensor(wlo[p0 % SPL][:, 0:n], raw[p0 % RAW][:, 0:n],
                              whi[p0 % SPL][:, 0:n].bitcast(F32), ALU.subtract).then_inc(lo_done, 1)

        def piece_ready(pe, p0, de=0):
            pe.wait_ge(lo_done, p0 + 1 + MOE_PIECES * de)

        def gain_src(n):
            if n == 8:
                g = final_norm
            else:
                g = (norm_mix if n % 2 == 0 else norm_ffn)[n // 2]
            return g.rearrange("(a d) -> a d", a=1).to_broadcast([P, D])

        def sp_program(sp):
            for t in range(TT):
                sp.dma_start(x[:, t, :], x_in[0].rearrange("(t p) d -> t p d", p=P)[t]).then_inc(x_in_s[t], 16)
            sp.dma_start(cst[:], consts).then_inc(cst_in, 16)
            for p0 in range(base["s5"] + RAW - 1):
                load_piece(sp, p0)
            s5_loads(sp)
            for p0 in range(base["s5"] + RAW - 1, base["moe0"]):
                load_piece(sp, p0)
            moe_loads(sp, 0)
            for p0 in range(base["mla"], base["moe1"]):
                load_piece(sp, p0)
            moe_loads(sp, 1)
            for t in range(TT):
                sp.wait_ge(nrm_h, TT * 8 + t + 1)
                sp.dma_start(out[0].rearrange("(t p) d -> t p d", p=P)[t], h[:, t, :]).then_inc(out_s, 16)
            sp.wait_ge(out_s, 16 * TT)

        def moe_loads(sp, m):
            b = base[f"moe{m}"]
            order = ffn_order(len(GU_E))

            def expert(e, de):
                for s, (kind, j) in enumerate(order):
                    c0, cw = GU_E[j]
                    if kind == "d":
                        src = moe_w_down[m, e, c0:c0 + cw, :] if type(e) is int else \
                            moe_w_down[m, bass.ds(e, 1), c0:c0 + cw, :].rearrange("a r n -> (a r) n")
                        src = src.rearrange("(k p) n -> p k n", p=P)
                    else:
                        c0 += FE if kind == "u" else 0
                        src = moe_w_gate_up[m, e, :, c0:c0 + cw] if type(e) is int else \
                            moe_w_gate_up[m, bass.ds(e, 1), :, c0:c0 + cw].rearrange("a r n -> (a r) n")
                        src = src.rearrange("(k p) n -> p k n", p=P)
                    load_piece(sp, b + s, src, de)

            with sp.Fori(0, NE) as e:
                expert(e, e)

        def x_ready(eng, n, t):
            if n == 0:
                eng.wait_ge(x_in_s[t], 16)
            else:
                eng.wait_ge(x_up, TT * (n - 1) + t + 1)

        STAGES = ["sb0", "dense0", "s5", "moe0", "mla", "dense1", "sb1", "moe1"]

        def held_back(n, count):
            return range(base[STAGES[n]] + SPL - count, base[STAGES[n]] + SPL) if 1 <= n < 8 else ()

        def norm_act(act, n):
            for t in range(TT):
                x_ready(act, n, t)
                act.activation(h[:, t, :], x[:, t, :], ACT.Square, accum_out=stat[:, 0, t:t + 1])\
                    .then_inc(nrm_sq, 1)
            for p0 in held_back(n, 1):
                split_hi(act, p0)
            if n == 8:
                return
            if n == 2:
                s5_prep_act(act)
            for j in range(4):
                act.wait_ge(nrm_tp, 4 * n + j + 1)
                if n == 2:
                    act.activation(s5m["hTf"][:, 2 * j:2 * j + 2, :].rearrange("p k l -> p (k l)"), PS[:, j, :],
                                   ACT.Copy).then_inc(nrm_hi, 1)
                else:
                    act.activation(hT_hi[:, 2 * j:2 * j + 2, :].rearrange("p k l -> p (k l)"), PS[:, j, :],
                                   ACT.Copy).then_inc(nrm_hi, 1)

        def norm_dve(dve, n):
            for t in range(TT):
                dve.wait_ge(nrm_sq, TT * n + t + 1)
                dve.tensor_scalar(stat[:, 1, t:t + 1], stat[:, 0, t:t + 1], 1.0 / D, EPS, ALU.mult, ALU.add)\
                    .then_inc(nrm_ms, 1)
            for t in range(TT):
                dve.wait_ge(nrm_rs, TT * n + t + 1)
                if t == 0:
                    dve.wait_ge(gain_in, 16 * (n + 1))
                dve.scalar_tensor_tensor(out=h[:, t, :], in0=x[:, t, :], scalar=stat[:, 2, t:t + 1],
                                         in1=gain[:], op0=ALU.mult, op1=ALU.mult).then_inc(nrm_h, 1)
            for j in range(4 if n not in (2, 8) else 0):
                dve.wait_ge(nrm_hi, 4 * n + j + 1)
                v = slice(2 * j, 2 * j + 2)
                dve.tensor_tensor(hT_lo[:, v, :].rearrange("p k l -> p (k l)"), PS[:, j, :],
                                  hT_hi[:, v, :].rearrange("p k l -> p (k l)").bitcast(F32), ALU.subtract)\
                    .then_inc(nrm_lo, 1)
            if n not in (3, 7):
                for p0 in held_back(n, 2):
                    split_lo(dve, p0)

        def norm_pool(pool, n):
            if n == 0:
                pool.wait_ge(cst_in, 16)
            for t in range(TT):
                pool.wait_ge(nrm_ms, TT * n + t + 1)
                pool.tensor_tensor(stat[:, 2, t:t + 1], stat[:, 1, t:t + 1], cst[:, C_POW:C_POW + 1],
                                   ALU.pow).then_inc(nrm_rs, 1)
            if n < 8:
                pool.wait_ge(nrm_h, TT * (n + 1))
                pool.dma_start(gain[:], gain_src(n + 1)).then_inc(gain_in, 16)

        def norm_pe(pe, n):
            if n == 0:
                pe.wait_ge(cst_in, 16)
            for t in range(TT):
                pe.wait_ge(nrm_h, TT * n + t + 1)
                for k in range(KC):
                    o = (k % 2) * L + t * P
                    i = pe.transpose(PS[:, k // 2, o:o + P], h[:, t, k * P:(k + 1) * P], ident)
                    if t == TT - 1 and k % 2:
                        i.then_inc(nrm_tp, 1)

        LOS = [0, 1, 2, 2, 3, 4, 5, 6]

        def hT_ready(pe, n):
            if n == 2:
                pe.wait_ge(nrm_hi, 4 * (n + 1))
            else:
                pe.wait_ge(nrm_lo, 4 * (LOS[n] + 1))

        def proj_pe(pe, b0):
            for i, (c0, w) in enumerate(DCOLS):
                p = b0 + i
                piece_ready(pe, p)
                wp = wpiece(p, KC, w)
                for t in range(TT):
                    for k in range(KC):
                        last = split3(pe, PS[:, 2 * i + t, 0:w], at((hT_hi, hT_lo), slice(None), k, slice(t * P, (t + 1) * P)),
                                      at(wp, slice(None), k, slice(None)), k == 0, k == KC - 1)
                last.then_inc(w_used, 1)

        def proj_dve(dve, b0):
            for i, (c0, w) in enumerate(DCOLS):
                dve.wait_ge(w_used, b0 + i + 1)
                for t in range(TT):
                    ins = dve.tensor_tensor(x[:, t, c0:c0 + w], x[:, t, c0:c0 + w], PS[:, 2 * i + t, 0:w], ALU.add)
                    if i == len(DCOLS) - 1:
                        ins.then_inc(x_up, 1)
                if i < len(DCOLS) - 2:
                    split_lo(dve, b0 + i + SPL)

        def proj_act(act, b0):
            for i in range(len(DCOLS) - 1):
                split_hi(act, b0 + i + SPL)

        at_q, at_k, at_va, at_vd = sem("at_q"), sem("at_k"), sem("at_va"), sem("at_vd")
        at_z, at_self, at_l, at_sp, at_m = (sem("at_z"), sem("at_self"), sem("at_l"),
                                                sem("at_sp"), sem("at_m"))
        at_c, at_w, at_wm, at_pv, at_oh, at_ol = (sem("at_c"), sem("at_w"), sem("at_wm"), sem("at_pv"),
                                                  sem("at_oh"), sem("at_ol"))
        NB = D // P
        QT, KT, VV = att["qT"], att["kT"], att["vv"]
        AZ, SP_, PW = [att["az0"], att["az1"]], [att["sp0"], att["sp1"]], [att["pw0"], att["pw1"]]

        QKB = ((4, 5, 6), (7, 2, 3))
        QKW = [w // P for _, w in DCOLS]

        def qk_bank(n, c):
            return PS[:, QKB[n % 2][c], 0:L]

        def zpair(i):
            return PS[:, 2 * (i % 3):2 * (i % 3) + 2, 0:384]

        def sb_pe(pe, a, n):
            b0 = base[f"sb{a}"]
            hT_ready(pe, n)
            for s in range(2):
                for i, (c0, w) in enumerate(DCOLS):
                    p = b0 + 3 * s + i
                    piece_ready(pe, p)
                    wp = wpiece(p, KC, w)
                    n = 3 * s + i
                    if n in (2, 3, 4):
                        pe.wait_ge(at_q, NB * a + sum(QKW[:n - 1]))
                    elif n == 5:
                        pe.wait_ge(at_k, NB * a + QKW[0])
                    for c in range(w // P):
                        for k in range(KC):
                            last = split3(pe, qk_bank(n, c), at(wp, slice(None), k, slice(c * P, (c + 1) * P)),
                                          at((hT_hi, hT_lo), slice(None), k, slice(None)), k == 0, k == KC - 1)
                    last.then_inc(w_used, 1)
            for i, (c0, w) in enumerate(DCOLS):
                p = b0 + 6 + i
                piece_ready(pe, p)
                wp = wpiece(p, KC, w)
                if i == 1:
                    pe.wait_ge(at_k, NB * (a + 1))
                if i == 2:
                    pe.wait_ge(at_va, 3 * a + 1)
                    pe.wait_ge(at_vd, 3 * a + 1)
                for t in range(TT):
                    for k in range(KC):
                        last = split3(pe, PS[:, (2 * i + t) % 4, 0:w],
                                      at((hT_hi, hT_lo), slice(None), k, slice(t * P, (t + 1) * P)),
                                      at(wp, slice(None), k, slice(None)), k == 0, k == KC - 1)
                last.then_inc(w_used, 1)

            def scores(i):
                if i == 0:
                    pe.wait_ge(at_q, NB * (a + 1))
                    pe.wait_ge(at_k, NB * (a + 1))
                    pe.wait_ge(at_va, 3 * (a + 1))
                    pe.wait_ge(at_vd, 3 * (a + 1))
                if i >= 3:
                    pe.wait_ge(at_w, PAIRS * a + i - 2)
                for j in range(2):
                    r = slice(j * HD, (j + 1) * HD)
                    z = PS[:, 2 * (i % 3) + j, :]
                    pe.matmul(z[:, 0:L], KT[r, i, 0:P], QT[r, i, 0:L], start=True, stop=False,
                              skip_group_check=True)
                    last = pe.matmul(z[:, L:L + P], KT[r, i, P:L], QT[r, i, P:L], start=False, stop=False,
                                     skip_group_check=True)
                last.then_inc(at_z, 1)

            def tails(i):
                pe.wait_ge(at_m, PAIRS * a + i + 1)
                sp = SP_[i % 2]
                for j in range(2):
                    z = PS[:, 2 * (i % 3) + j, :]
                    pe.matmul(z[:, 0:L], negtri, sp[:, j, 0:L], start=False, stop=False, skip_group_check=True)
                    pe.matmul(z[:, P:L], negone, sp[:, j, L:L + P], start=False, stop=False, skip_group_check=True)
                    last = pe.matmul(z[:, L:L + P], negtri, sp[:, j, L:L + P], start=False, stop=True,
                                     skip_group_check=True)
                last.then_inc(at_c, 1)

            def values(i):
                pe.wait_ge(at_wm, PAIRS * a + i + 1)
                if i >= 2:
                    pe.wait_ge(at_ol, PAIRS * a + i - 1)
                if a == 0 and i == 0:
                    pe.wait_ge(s5_parE, 1)
                w = PW[i % 2]
                for j in range(2):
                    r = slice(j * HD, (j + 1) * HD)
                    c = slice((2 * i + j) * HD, (2 * i + j + 1) * HD)
                    o = PS[r, 6 + i % 2, 0:L]
                    pe.matmul(o, VV[:, 0, c], w[:, j, 0:L], start=True, stop=False, skip_group_check=True)
                    last = pe.matmul(o[:, P:L], VV[:, 1, c], w[:, j, L:L + P], start=False, stop=True,
                                     skip_group_check=True)
                last.then_inc(at_pv, 1)

            if a == 0:
                s5_par_pe(pe)
            for i in range(PAIRS + 2):
                if i < PAIRS:
                    scores(i)
                if 1 <= i <= PAIRS:
                    tails(i - 1)
                if i >= 2:
                    values(i - 2)
            pe.wait_ge(at_ol, PAIRS * (a + 1))
            proj_pe(pe, b0 + 9)

        def sb_act(act, a, n):
            b0 = base[f"sb{a}"]
            for i, (c0, w) in enumerate(DCOLS):
                act.wait_ge(w_used, b0 + i + 1)
                split_hi(act, b0 + i + SPL)
                for c in range(w // P):
                    b = c0 // P + c
                    act.activation(QT[:, b, :], qk_bank(i, c), ACT.Copy, scale=HD ** -0.5).then_inc(at_q, 1)
            for i in range(3):
                split_hi(act, b0 + 3 + i + SPL)
            for i, (c0, w) in enumerate(DCOLS):
                act.wait_ge(w_used, b0 + 6 + i + 1)
                split_hi(act, b0 + 6 + i + SPL)
                act.activation(VV[:, 0, c0:c0 + w], PS[:, (2 * i) % 4, 0:w], ACT.Copy).then_inc(at_va, 1)
            if a == 0:
                s5_par_act(act)
            act.preload_act_table_set("natural_log_exp_and_others")
            for i in range(PAIRS + 2):
                if i < PAIRS:
                    z = AZ[i % 2][:].rearrange("p a b -> p (a b)")
                    act.wait_ge(at_z, PAIRS * a + i + 1)
                    act.activation(AZ[i % 2][:], zpair(i), ACT.Abs).then_inc(at_self, 1)
                    act.wait_ge(at_self, 2 * (PAIRS * a + i) + 1)
                    act.activation(z, z, ACT.Exp, scale=-1.0).then_inc(at_self, 1)
                    act.wait_ge(at_self, 2 * (PAIRS * a + i) + 2)
                    act.activation(z, z, ACT.Ln, bias=1.0).then_inc(at_l, 1)
                if 1 <= i <= PAIRS:
                    k = i - 1
                    act.wait_ge(at_c, PAIRS * a + k + 1)
                    if k >= 2:
                        act.wait_ge(at_pv, PAIRS * a + k - 1)
                    act.activation(PW[k % 2][:], zpair(k), ACT.Exp).then_inc(at_w, 1)
                if i >= 2:
                    k = i - 2
                    act.wait_ge(at_pv, PAIRS * a + k + 1)
                    act.activation(hT_hi[:, k, :], PS[:, 6 + k % 2, 0:L], ACT.Copy).then_inc(at_oh, 1)
            proj_act(act, b0 + 9)

        def sb_dve(dve, a, n):
            b0 = base[f"sb{a}"]
            for i in range(3):
                split_lo(dve, b0 + i + SPL)
            for i, (c0, w) in enumerate(DCOLS):
                dve.wait_ge(w_used, b0 + 3 + i + 1)
                for c in range(w // P):
                    b = c0 // P + c
                    dve.tensor_copy(KT[:, b, :], qk_bank(3 + i, c)).then_inc(at_k, 1)
                split_lo(dve, b0 + 3 + i + SPL)
            for i, (c0, w) in enumerate(DCOLS):
                dve.wait_ge(w_used, b0 + 6 + i + 1)
                dve.tensor_copy(VV[:, 1, c0:c0 + w], PS[:, (2 * i + 1) % 4, 0:w]).then_inc(at_vd, 1)
                split_lo(dve, b0 + 6 + i + SPL)
            for i in range(PAIRS + 2):
                if i < PAIRS:
                    dve.wait_ge(at_l, PAIRS * a + i + 1)
                    if i >= 2:
                        dve.wait_ge(at_c, PAIRS * a + i - 1)
                    dve.scalar_tensor_tensor(out=SP_[i % 2][:], in0=zpair(i), scalar=0.0, in1=AZ[i % 2][:],
                                             op0=ALU.max, op1=ALU.add).then_inc(at_sp, 1)
                if i >= 2:
                    k = i - 2
                    dve.wait_ge(at_oh, PAIRS * a + k + 1)
                    dve.tensor_tensor(hT_lo[:, k, :], PS[:, 6 + k % 2, 0:L], hT_hi[:, k, :].bitcast(F32),
                                      ALU.subtract).then_inc(at_ol, 1)
            proj_dve(dve, b0 + 9)

        def sb_pool(pool, a, n):
            def strict(t):
                for j in range(2):
                    v = t[:, j, :].rearrange("p (c q) -> p c q", q=P)[:, 0:3:2, :]
                    last = pool.affine_select(out=v, in_=v, compare_op=ALU.is_gt, fill=0.0, base=0,
                                              pattern=[[0, 2], [1, P]], channel_multiplier=-1)
                return last
            for i in range(PAIRS + 1):
                if i < PAIRS:
                    pool.wait_ge(at_sp, PAIRS * a + i + 1)
                    strict(SP_[i % 2]).then_inc(at_m, 1)
                if i >= 1:
                    pool.wait_ge(at_w, PAIRS * a + i)
                    strict(PW[(i - 1) % 2]).then_inc(at_wm, 1)

        f_silu, f_mul, f_tp, f_hi, f_lo = sem("f_silu"), sem("f_mul"), sem("f_tp"), sem("f_hi"), sem("f_lo")
        JD = len(GU_D)
        AHI, ALO = [ff["ahi0"], ff["ahi1"]], [ff["alo0"], ff["alo1"]]

        def numbered(n):
            return {key: s for s, key in enumerate(ffn_order(n))}

        ND, NX = numbered(JD), numbered(len(GU_E))

        def dense_pe(pe, f, n):
            b0 = base[f"dense{f}"]
            hT_ready(pe, n)

            def gate_or_up(kind, j):
                p, w = b0 + ND[kind, j], GU_D[j][1]
                piece_ready(pe, p)
                wp = wpiece(p, KC, w)
                bank = 0 if kind == "g" else 2
                for t in range(TT):
                    for k in range(KC):
                        last = split3(pe, PS[:, bank + t, 0:w],
                                      at((hT_hi, hT_lo), slice(None), k, slice(t * P, (t + 1) * P)),
                                      at(wp, slice(None), k, slice(None)), k == 0, k == KC - 1)
                last.then_inc(w_used, 1)

            for j in range(JD + 2):
                if j < JD:
                    if j >= 1:
                        pe.wait_ge(f_silu, JD * f + j)
                    gate_or_up("g", j)
                if 1 <= j <= JD:
                    pe.wait_ge(f_mul, JD * f + j)
                    for c in range(GU_D[j - 1][1] // P):
                        for t in range(TT):
                            o = 2 * 512 + c * L + t * P
                            last = pe.transpose(psf[:, o:o + P], ff["act"][:, t, c * P:(c + 1) * P], ident)
                    last.then_inc(f_tp, 1)
                if j >= 2:
                    i = j - 2
                    p, kc = b0 + ND["d", i], GU_D[i][1] // P
                    piece_ready(pe, p)
                    pe.wait_ge(f_lo, JD * f + i + 1)
                    wp = wpiece(p, kc, D)
                    for t in range(TT):
                        for half in range(2):
                            for c in range(kc):
                                s = slice(c * L + t * P, c * L + (t + 1) * P)
                                last = split3(pe, PS[:, 4 + 2 * t + half, :], (AHI[i % 2][:, s], ALO[i % 2][:, s]),
                                              at(wp, slice(None), c, slice(half * 512, half * 512 + 512)),
                                              i == 0 and c == 0, i == JD - 1 and c == kc - 1)
                    last.then_inc(w_used, 1)
                if j < JD:
                    if j >= 1:
                        pe.wait_ge(f_lo, JD * f + j)
                    gate_or_up("u", j)

        def dense_act(act, f, n):
            b0 = base[f"dense{f}"]
            for j in range(JD + 2):
                if j < JD:
                    p, w = b0 + ND["g", j], GU_D[j][1]
                    act.wait_ge(w_used, p + 1)
                    if j >= 1:
                        act.wait_ge(f_mul, JD * f + j)
                    act.activation(ff["sg"][:, :, 0:w], PS[:, 0:2, 0:w], ACT.Silu).then_inc(f_silu, 1)
                    split_hi(act, p + SPL)
                if 1 <= j <= JD:
                    m = GU_D[j - 1][1] // P * L
                    act.wait_ge(f_tp, JD * f + j)
                    act.activation(AHI[(j - 1) % 2][:, 0:m], psf[:, 1024:1024 + m], ACT.Copy).then_inc(f_hi, 1)
                if 2 <= j < JD + 1:
                    split_hi(act, b0 + ND["d", j - 2] + SPL)
                if j < JD:
                    split_hi(act, b0 + ND["u", j] + SPL)

        def dense_dve(dve, f, n):
            b0 = base[f"dense{f}"]
            for j in range(JD + 2):
                if 1 <= j <= JD:
                    m = GU_D[j - 1][1] // P * L
                    if j < JD:
                        split_lo(dve, b0 + ND["g", j] + SPL)
                    dve.wait_ge(f_hi, JD * f + j)
                    dve.tensor_tensor(ALO[(j - 1) % 2][:, 0:m], psf[:, 1024:1024 + m],
                                      AHI[(j - 1) % 2][:, 0:m].bitcast(F32), ALU.subtract).then_inc(f_lo, 1)
                elif j == 0:
                    split_lo(dve, b0 + ND["g", j] + SPL)
                if 2 <= j < JD:
                    split_lo(dve, b0 + ND["d", j - 2] + SPL)
                if j < JD:
                    p, w = b0 + ND["u", j], GU_D[j][1]
                    dve.wait_ge(w_used, p + 1)
                    dve.wait_ge(f_silu, JD * f + j + 1)
                    dve.tensor_tensor(ff["act"][:, :, 0:w], PS[:, 2:4, 0:w], ff["sg"][:, :, 0:w], ALU.mult)\
                        .then_inc(f_mul, 1)
                    split_lo(dve, p + SPL)
            dve.wait_ge(w_used, b0 + 3 * JD)
            for t in range(TT):
                dve.tensor_tensor(x[:, t, :], x[:, t, :], psf[:, (4 + 2 * t) * 512:(6 + 2 * t) * 512], ALU.add)\
                    .then_inc(x_up, 1)

        s5_ld, s5_a, s5_g, s5_rows, s5_parT, s5_parE = (sem("s5_ld"), sem("s5_a"), sem("s5_g"), sem("s5_rows"),
                                                        sem("s5_parT"), sem("s5_parE"))
        s5_nat, s5_pad = sem("s5_nat"), sem("s5_pad")
        s5_tw = [sem("s5_tw0"), sem("s5_tw1")]
        s5_ti = [sem(f"s5_ti{i}") for i in range(4)]
        s5_bt, s5_be, s5_ctt, s5_cte = sem("s5_bt"), sem("s5_be"), sem("s5_ctt"), sem("s5_cte")
        s5_in, s5_bu, s5_vi, s5_zi, s5_u, s5_c = (sem("s5_in"), sem("s5_bu"), sem("s5_vi"), sem("s5_zi"),
                                                  sem("s5_u"), sem("s5_c"))
        s5_y, s5_ge, s5_yh, s5_yl, s5_sg, s5_pr = (sem("s5_y"), sem("s5_ge"), sem("s5_yh"), sem("s5_yl"),
                                                   sem("s5_sg"), sem("s5_pr"))
        TAB_PIECE = base["s5"] + RAW - 1
        TABS = raw[TAB_PIECE % RAW][:].rearrange("p (b a l) -> p b a l", b=4, a=3)
        R = setup["r_w"]
        r_dtb = setup["r_dt"][:].rearrange("t (g a) -> t g a", a=1).to_broadcast([ST, 2, SS])

        def row(i):
            return R[:, i, :]

        def row2(i):
            return R[:, i, :].rearrange("t (g p) -> t g p", g=2)

        LRDT, ANG, KK, RED, TMP, ABS, A_RE, A_IM, DEN, MAG, CO, SI, F_RE, F_IM = range(14)
        RG = [0]

        def glink(pool, ins):
            RG[0] += 1
            ins.then_inc(chain_g, 1)
            pool.wait_ge(chain_g, RG[0])

        def s5_setup_pool(pool):
            pool.dma_start(gain[:], gain_src(0)).then_inc(gain_in, 16)
            pool.dma_start(setup["r_lr"][:], lam_re_in[0].rearrange("(t g) p -> t (g p)", g=2)).then_inc(s5_ld, 16)
            pool.dma_start(setup["r_li"][:], lam_im_in[0].rearrange("(t g) p -> t (g p)", g=2)).then_inc(s5_ld, 16)
            pool.dma_start(setup["r_ldt"][:], log_dt_in[0].rearrange("(t g) -> t g", g=2)).then_inc(s5_ld, 16)

        def s5_setup_pool2(pool):
            lr, li = setup["r_lr"], setup["r_li"]
            g2 = lambda t: t[:].rearrange("t (g p) -> t g p", g=2)
            pool.wait_ge(cst_in, 16)
            pool.wait_ge(s5_a, 1)
            glink(pool, pool.tensor_tensor(row2(LRDT), g2(lr), r_dtb, ALU.mult))
            glink(pool, pool.tensor_tensor(row2(ANG), g2(li), r_dtb, ALU.mult))
            magic = float(1.5 * 2 ** 23)
            glink(pool, pool.tensor_scalar(row(TMP), row(ANG), 1.0 / TWO_PI, None, ALU.mult))
            glink(pool, pool.tensor_scalar(row(KK), row(TMP), magic, None, ALU.add))
            glink(pool, pool.tensor_scalar(row(TMP), row(KK), -magic, None, ALU.add))
            src = ANG
            for c in (PI_A, PI_B, PI_C):
                glink(pool, pool.tensor_scalar(row(KK), row(TMP), c, None, ALU.mult))
                glink(pool, pool.tensor_tensor(row(RED), row(src), row(KK), ALU.subtract))
                src = RED
            pool.tensor_scalar(row(RED), row(RED), PI_MAX, -PI_MAX, ALU.min, ALU.max).then_inc(s5_g, 1)
            pool.wait_ge(s5_a, 5)
            glink(pool, pool.tensor_tensor(row(A_RE), row(MAG), row(CO), ALU.mult))
            glink(pool, pool.tensor_tensor(row(A_IM), row(MAG), row(SI), ALU.mult))
            glink(pool, pool.tensor_scalar(row(A_RE), row(A_RE), -1.0, None, ALU.add))
            glink(pool, pool.tensor_tensor(row(DEN), lr[:], lr[:], ALU.mult))
            glink(pool, pool.tensor_tensor(row(TMP), li[:], li[:], ALU.mult))
            glink(pool, pool.tensor_tensor(row(DEN), row(DEN), row(TMP), ALU.add))
            glink(pool, pool.tensor_tensor(row(DEN), row(DEN), cst[0:ST, C_POW + 1:C_POW + 2].to_broadcast([ST, P]),
                                           ALU.pow))
            glink(pool, pool.tensor_tensor(row(TMP), row(A_RE), lr[:], ALU.mult))
            glink(pool, pool.tensor_tensor(row(KK), row(A_IM), li[:], ALU.mult))
            glink(pool, pool.tensor_tensor(row(TMP), row(TMP), row(KK), ALU.add))
            glink(pool, pool.tensor_tensor(row(F_RE), row(TMP), row(DEN), ALU.mult))
            glink(pool, pool.tensor_tensor(row(TMP), row(A_IM), lr[:], ALU.mult))
            glink(pool, pool.tensor_tensor(row(KK), row(A_RE), li[:], ALU.mult))
            glink(pool, pool.tensor_tensor(row(TMP), row(TMP), row(KK), ALU.subtract))
            pool.tensor_tensor(row(F_IM), row(TMP), row(DEN), ALU.mult).then_inc(s5_rows, 1)

        def s5_setup_act(act):
            act.wait_ge(s5_ld, 48)
            act.activation(setup["r_dt"][:], setup["r_ldt"][:], ACT.Exp).then_inc(s5_a, 1)

        def s5_setup_act2(act):
            act.wait_ge(s5_g, 1)
            act.activation(row(MAG), row(LRDT), ACT.Exp).then_inc(s5_a, 1)
            act.activation(row(SI), row(RED), ACT.Sin).then_inc(s5_a, 1)
            act.activation(row(ABS), row(RED), ACT.Abs).then_inc(s5_a, 1)
            act.wait_ge(s5_a, 4)
            act.wait_ge(cst_in, 16)
            act.activation(row(CO), row(ABS), ACT.Sin, scale=-1.0, bias=cst[0:ST, C_POW + 2:C_POW + 3]).then_inc(s5_a, 1)

        def s5_par_pe(pe):
            pe.wait_ge(s5_rows, 1)
            for q, src in enumerate((MAG, CO, SI, F_RE, F_IM)):
                last = pe.transpose(PS[:, 6, q * ST:(q + 1) * ST], row(src), ident[0:ST, 0:ST])
            last.then_inc(s5_parT, 1)

        def s5_par_act(act):
            act.wait_ge(s5_parT, 1)
            act.activation(s5_par[:].rearrange("p a t -> p (a t)"), PS[:, 6, 0:5 * ST], ACT.Copy)\
                .then_inc(s5_parE, 1)

        def s5_tables_pool(pool):
            tc, ts_, uc, us = ff["ta_c"], ff["ta_s"], ff["tb_c"], ff["tb_s"]
            a_, b_ = ff["tm0"][:].rearrange("p a b -> p (a b)"), ff["tm1"][:].rearrange("p a b -> p (a b)")
            pool.wait_ge(s5_parE, 1)
            wc, ws, nc_, ns = (pk[:, i, :] for i in range(4))
            glink(pool, pool.tensor_copy(wc, s5_par[:, 1, :]))
            glink(pool, pool.tensor_copy(ws, s5_par[:, 2, :]))
            for c_, s_ in ((tc, ts_), (uc, us)):
                pool.memset(c_[:, :, 0:1], 1.0)
                glink(pool, pool.memset(s_[:, :, 0:1], 0.0))
                for j in range(4):
                    n = 2 ** j
                    lo, up = slice(0, n), slice(n, 2 * n)
                    v = lambda t, o: t[:, o:o + ST * n].rearrange("p (t n) -> p t n", n=n)
                    bc = wc.rearrange("p (t a) -> p t a", a=1).to_broadcast([P, ST, n])
                    bs = ws.rearrange("p (t a) -> p t a", a=1).to_broadcast([P, ST, n])
                    pool.tensor_tensor(v(a_, 0), c_[:, :, lo], bc, ALU.mult)
                    pool.tensor_tensor(v(a_, 256), s_[:, :, lo], bs, ALU.mult)
                    pool.tensor_tensor(v(b_, 0), c_[:, :, lo], bs, ALU.mult)
                    glink(pool, pool.tensor_tensor(v(b_, 256), s_[:, :, lo], bc, ALU.mult))
                    pool.tensor_tensor(c_[:, :, up], v(a_, 0), v(a_, 256), ALU.subtract)
                    glink(pool, pool.tensor_tensor(s_[:, :, up], v(b_, 0), v(b_, 256), ALU.add))
                    pool.tensor_tensor(nc_, wc, wc, ALU.mult)
                    pool.tensor_tensor(ns, ws, ws, ALU.mult)
                    glink(pool, pool.tensor_tensor(a_[:, 0:ST], wc, ws, ALU.mult))
                    pool.tensor_tensor(wc, nc_, ns, ALU.subtract)
                    glink(pool, pool.tensor_scalar(ws, a_[:, 0:ST], 2.0, None, ALU.mult))
            for i in range(ST // 2):
                tg = ff[f"tg{i % 2}"]
                t2 = slice(2 * i, 2 * i + 2)
                q4 = lambda t: t.rearrange("p t (a b) -> p t a b", a=16)
                A = lambda t: t[:, t2, :].rearrange("p t (o b) -> p t o b", o=1).to_broadcast([P, 2, 16, 16])
                B = lambda t: t[:, t2, :].rearrange("p t (a o) -> p t a o", o=1).to_broadcast([P, 2, 16, 16])
                m0, m1 = q4(ff["tm0"][:]), q4(ff["tm1"][:])
                if i >= 2:
                    pool.wait_ge(s5_tw[i % 2], 16 * (i // 2))
                pool.tensor_tensor(m0, A(tc), B(uc), ALU.mult)
                glink(pool, pool.tensor_tensor(m1, A(ts_), B(us), ALU.mult))
                glink(pool, pool.tensor_tensor(q4(tg[:, :, 0, :]), m0, m1, ALU.subtract))
                pool.tensor_tensor(m0, A(ts_), B(uc), ALU.mult)
                glink(pool, pool.tensor_tensor(m1, A(tc), B(us), ALU.mult))
                glink(pool, pool.tensor_tensor(q4(tg[:, :, 1, :]), m0, m1, ALU.add))
                pool.dma_start(tabs[t2].rearrange("t p n -> p t n"), tg[:].rearrange("p t a n -> p t (a n)"))\
                    .then_inc(s5_tw[i % 2], 16)

        def s5_mats_pool(pool):
            bn, bp, cn_ = s5p["bnat"], s5p["bpad"], s5p["cnat"]
            tmp = s5p["btmp"]
            for b in range(2):
                pool.wait_ge(s5_tw[b], 16 * (ST // 4))
            glink(pool, pool.memset(bp[:], 0.0))
            glink(pool, pool.memset(cn_[:], 0.0))
            for q, src in enumerate((b_re_in, b_im_in)):
                for g in range(2):
                    pool.dma_start(bn[g * SS:(g + 1) * SS, q], src[0].rearrange("(t g) p c -> g p t c", g=2)[g])\
                        .then_inc(s5_nat, 16)
            for q, src in enumerate((c_re_in, c_im_in)):
                for g in range(KC):
                    pool.dma_start(cn_[g * SG:(g + 1) * SG, q, :, (g % 2) * SS:(g % 2 + 1) * SS],
                                   src[0].rearrange("(k g) c p -> g c k p", g=KC)[g]).then_inc(s5_nat, 16)
            pool.dma_start(s5p["dnat"][:], s5_d[0].rearrange("(k p) -> k p", p=P)).then_inc(s5_nat, 16)
            pool.wait_ge(s5_nat, 16 * (4 + 2 * KC + 1))
            fr = s5_par[:, 3, :].rearrange("p (t a) -> p t a", a=1).to_broadcast([P, ST, SG])
            fi = s5_par[:, 4, :].rearrange("p (t a) -> p t a", a=1).to_broadcast([P, ST, SG])
            for q, (op, f0, f1) in enumerate(((ALU.subtract, fr, fi), (ALU.add, fi, fr))):
                pool.tensor_tensor(tmp[:, 0], bn[:, 0], f0, ALU.mult)
                glink(pool, pool.tensor_tensor(tmp[:, 1], bn[:, 1], f1, ALU.mult))
                for g in range(2):
                    r = slice(g * SS, (g + 1) * SS)
                    last = pool.tensor_tensor(bp[r, q, :, g, :], tmp[r, 0], tmp[r, 1], op)
                if q == 0:
                    glink(pool, last)
            last.then_inc(s5_pad, 1)
            pool.wait_ge(s5_pad, 1)

        def s5_prep_pe(pe):
            pe.wait_ge(s5_pad, 1)
            pe.wait_ge(x_up, 4)
            for k in range(KC):
                for q in range(2):
                    src = s5p["bpad"][:, q, 4 * k:4 * k + 4, :, :].rearrange("p t g c -> p (t g c)")
                    last = pe.transpose(psf[:, 2048 + (2 * k + q) * P:2048 + (2 * k + q + 1) * P], src, ident)
            last.then_inc(s5_bt, 1)

        def s5_prep_act(act):
            act.wait_ge(s5_bt, 1)
            for b in range(4):
                ins = act.activation(s5m["bbt"][:, 2 * b:2 * b + 2].rearrange("p k q s -> p (k q s)"), PS[:, 4 + b, :],
                                     ACT.Copy)
            ins.then_inc(s5_be, 1)

        def s5_pe(pe):
            pe.wait_ge(s5_be, 1)
            for q in range(2):
                for k in range(KC):
                    o = 2048 + (q * KC + k) * P
                    pe.transpose(psf[:, o:o + P], s5p["cnat"][:, q, k, :], ident)
            pe.wait_ge(nrm_hi, 4 * 3)
            pe.transpose(PS[:, 0, 0:KC], s5p["dnat"][:], ident[0:KC, 0:KC]).then_inc(s5_ctt, 1)
            bbt, ct = s5m["bbt"], s5m["ct"]
            pe.wait_ge(s5_cte, 1)

            def inputs(t):
                k, j = t // 4, t % 4
                r = slice(32 * j, 32 * j + 32)
                if t >= 4:
                    pe.wait_ge(s5_bu, t - 3)
                pe.matmul(PS[:, t % 4, 0:L], bbt[r, k, 0, :], s5m["hTf"][r, k, :], start=True, stop=True,
                          skip_group_check=True)
                pe.matmul(PS[:, t % 4, L:2 * L], bbt[r, k, 1, :], s5m["hTf"][r, k, :], start=True, stop=True,
                          skip_group_check=True).then_inc(s5_in, 1)

            def outputs(t):
                k, j = t // 4, t % 4
                if k >= 2 and j == 0:
                    pe.wait_ge(s5_y, k - 1)
                pe.wait_ge(s5_u, t + 1)
                o = PS[32 * j:32 * j + 32, 4 + k % 2, 0:L]
                for q, m in enumerate((0, 1, 2, 2)):
                    last = pe.matmul(o, ct[:, k, m, 32 * j:32 * j + 32], s5m["uu"][:, q, :], start=(q == 0),
                                     stop=(q == 3), skip_group_check=True)
                last.then_inc(s5_c, 1)

            for t in range(ST + 3):
                if t < ST:
                    inputs(t)
                if t >= 3:
                    outputs(t - 3)
            pe.wait_ge(s5_yl, KC)
            b0 = base["s5"]
            for i, (c0, w) in enumerate(DCOLS):
                for q in range(2):
                    p = b0 + 2 * i + q
                    piece_ready(pe, p)
                    if i == 2 and q == 0:
                        pe.wait_ge(s5_pr, 1)
                    wp = wpiece(p, KC, w)
                    for t in range(TT):
                        for k in range(KC):
                            last = split3(pe, PS[:, 4 * (i % 2) + 2 * q + t, 0:w],
                                          at((hT_hi, hT_lo), slice(None), k, slice(t * P, (t + 1) * P)),
                                          at(wp, slice(None), k, slice(None)), k == 0, k == KC - 1)
                    last.then_inc(w_used, 1)

        def s5_act(act):
            act.wait_ge(s5_ctt, 1)
            ct = s5m["ct"]
            for m, (q, s) in enumerate(((0, 1.0), (0, -1.0), (1, -1.0))):
                for b in range(2):
                    act.activation(ct[:, 4 * b:4 * b + 4, m, :], PS[:, 4 + 2 * q + b, :].rearrange("p (k s) -> p k s", k=4),
                                   ACT.Copy, scale=s)
            act.activation(dT[:], PS[:, 0, 0:KC], ACT.Copy).then_inc(s5_cte, 1)
            for t in range(ST + 6):
                if t < ST:
                    act.wait_ge(s5_in, t + 1)
                    if t >= 4:
                        act.wait_ge(s5_u, t - 3)
                        act.wait_ge(s5_vi, t - 3)
                    act.activation(s5m[f"bu{t % 4}"][:].rearrange("p a l -> p (a l)"), PS[:, t % 4, :], ACT.Copy)\
                        .then_inc(s5_bu, 1)
                if t >= 9 and t % 4 == 1:
                    k = (t - 9) // 4
                    y = s5m["yt"][:, k % 2, :]
                    act.wait_ge(s5_y, k + 1)
                    act.activation(y, y, ACT.Gelu_apprx_tanh).then_inc(s5_ge, 1)
                    act.wait_ge(s5_ge, k + 1)
                    act.activation(hT_hi[:, k, :], y, ACT.Copy).then_inc(s5_yh, 1)
            b0 = base["s5"]
            for i, (c0, w) in enumerate(DCOLS):
                split_hi(act, b0 + 2 * i + SPL)
                act.wait_ge(w_used, b0 + 2 * i + 2)
                if i >= 1:
                    act.wait_ge(s5_pr, i)
                g = 4 * (i % 2) + 2
                act.activation(s5g["sgl"][:, :, 0:w], PS[:, g:g + 2, 0:w], ACT.Sigmoid).then_inc(s5_sg, 1)
                if i < len(DCOLS) - 1:
                    split_hi(act, b0 + 2 * i + 1 + SPL)

        def s5_dve(dve):
            vk = [0]

            def link(ins):
                vk[0] += 1
                ins.then_inc(chain_v, 1)
                dve.wait_ge(chain_v, vk[0])

            def chunk(k):
                dve.wait_ge(s5_c, 4 * k + 4)
                if k == 0:
                    dve.wait_ge(s5_cte, 1)
                if k >= 2:
                    dve.wait_ge(s5_yl, k - 1)
                dve.scalar_tensor_tensor(out=s5m["yt"][:, k % 2, :], in0=s5m["hTf"][:, k, :],
                                         scalar=dT[:, k:k + 1], in1=PS[:, 4 + k % 2, 0:L],
                                         op0=ALU.mult, op1=ALU.add).then_inc(s5_y, 1)

            def low(k):
                dve.wait_ge(s5_yh, k + 1)
                dve.tensor_tensor(hT_lo[:, k, :], s5m["yt"][:, k % 2, :], hT_hi[:, k, :].bitcast(F32), ALU.subtract)\
                    .then_inc(s5_yl, 1)

            zz, vv, m12, uu = (s5m["zz"], s5m["zz1"]), s5m["vvv"], s5m["m12"], s5m["uu"]

            def turn_back(t, part):
                if part == 0:
                    dve.wait_ge(s5_zi, t + 1)
                    if t >= 1:
                        dve.wait_ge(s5_c, t)
                last = dve.tensor_tensor(uu[:, 2 * part:2 * part + 2, :], zz[t % 2][:],
                                         TABS[:, t % 4, part:part + 2, :], ALU.mult)
                if part == 1:
                    last.then_inc(s5_u, 1)

            for t in range(ST + 7):
                if t < ST:
                    mag = s5_par[:, 0, t:t + 1].to_broadcast([P, L])
                    dve.wait_ge(s5_bu, t + 1)
                    dve.wait_ge(s5_ti[t % 4], 32 * (t // 4 + 1))
                    dve.tensor_tensor(m12[:], s5m[f"bu{t % 4}"][:], TABS[:, t % 4, 0:2, :], ALU.mult)\
                        .then_inc(chain_v, 1)
                    vk[0] += 1
                if 1 <= t <= ST:
                    turn_back(t - 1, 0)
                if t < ST:
                    dve.wait_ge(chain_v, vk[0])
                    dve.tensor_tensor(vv[:, 0, :], m12[:, 0, :], m12[:, 1, :], ALU.add).then_inc(chain_v, 1)
                    vk[0] += 1
                if 1 <= t <= ST:
                    turn_back(t - 1, 1)
                if t < ST:
                    dve.wait_ge(chain_v, vk[0])
                    dve.tensor_tensor_scan(zz[t % 2][:, 0, :], mag, vv[:, 0, :], 0.0, ALU.mult, ALU.add)
                    dve.wait_ge(s5_vi, t + 1)
                    dve.tensor_tensor_scan(zz[t % 2][:, 1, :], mag, vv[:, 1, :], 0.0, ALU.mult, ALU.add)\
                        .then_inc(s5_zi, 1)
                if t >= 7 and (t - 7) % 4 == 0 and (t - 7) // 4 < KC:
                    chunk((t - 7) // 4)
                if t >= 10 and (t - 10) % 4 == 0 and (t - 10) // 4 < KC:
                    low((t - 10) // 4)
            b0 = base["s5"]
            for i, (c0, w) in enumerate(DCOLS):
                if i < len(DCOLS) - 1:
                    split_lo(dve, b0 + 2 * i + SPL)
                dve.wait_ge(s5_sg, i + 1)
                v = 4 * (i % 2)
                dve.tensor_tensor(s5g["prod"][:, :, 0:w], PS[:, v:v + 2, 0:w], s5g["sgl"][:, :, 0:w], ALU.mult)\
                    .then_inc(s5_pr, 1)
                dve.wait_ge(s5_pr, i + 1)
                for t in range(TT):
                    ins = dve.tensor_tensor(x[:, t, c0:c0 + w], x[:, t, c0:c0 + w], s5g["prod"][:, t, 0:w], ALU.add)
                    if i == len(DCOLS) - 1:
                        ins.then_inc(x_up, 1)
                if i < len(DCOLS) - 1:
                    link(ins)
                    split_lo(dve, b0 + 2 * i + 1 + SPL)

        def s5_pool(pool):
            m34, vv = s5m["m34"], s5m["vvv"]
            for t in range(ST):
                bu, tab = s5m[f"bu{t % 4}"], TABS[:, t % 4]
                pool.wait_ge(s5_bu, t + 1)
                pool.wait_ge(s5_ti[t % 4], 32 * (t // 4 + 1))
                if t >= 1:
                    pool.wait_ge(s5_vi, t)
                glink(pool, pool.tensor_tensor(m34[:], bu[:], tab[:, 1:3, :], ALU.mult))
                if t >= 1:
                    pool.wait_ge(s5_zi, t)
                pool.tensor_tensor(vv[:, 1, :], m34[:, 1, :], m34[:, 0, :], ALU.subtract).then_inc(s5_vi, 1)

        def s5_loads(sp):
            for b in range(2):
                sp.wait_ge(s5_tw[b], 16 * (ST // 4))
            sp.wait_ge(lo_done, TAB_PIECE - RAW + 1)
            for t in range(ST):
                if t >= 4:
                    sp.wait_ge(s5_u, t - 3)
                    sp.wait_ge(s5_vi, t - 3)
                tab = TABS[:, t % 4]
                sp.dma_start(tab[:, 0:2, :].rearrange("p a l -> p (a l)"), tabs[t]).then_inc(s5_ti[t % 4], 16)
                sp.dma_start(tab[:, 2, :], tabs[t][:, 0:L]).then_inc(s5_ti[t % 4], 16)
            sp.wait_ge(s5_u, ST)
            sp.wait_ge(s5_vi, ST)

        m_wr, m_hh, m_hl, m_wh, m_wl, m_lg, m_sel, m_gd, m_ge, m_rk = (
            sem("m_wr"), sem("m_hh"), sem("m_hl"), sem("m_wh"), sem("m_wl"), sem("m_lg"), sem("m_sel"), sem("m_gd"),
            sem("m_ge"), sem("m_rk"))
        m_lt, m_lc, m_ovf = sem("m_lt"), sem("m_lc"), sem("m_ovf")
        chain_m = sem("chain_m")

        class ExpertSems:
            def __init__(self):
                self.silu = sem("x_silu")
                self.mul = sem("x_mul")
                self.tp = sem("x_tp")
                self.ahi = sem("x_ahi")
                self.alo = sem("x_alo")
                self.gr = sem("x_gr")
                self.copied = sem("x_gc")
                self.g = sem("x_g")
                self.ghi = sem("x_ghi")
                self.glo = sem("x_glo")
                self.sc = sem("x_sc")
                self.xa = sem("x_xa")
                self.pt = sem("x_pt")
                self.put = sem("x_put")
                self.yhi = sem("x_yhi")
                self.ylo = sem("x_ylo")
                self.pick = sem("x_pick")
                self.cur = sem("x_cur")
                self.cug = sem("x_cug")

        ex = ExpertSems()
        JE = len(GU_E)
        MHI, MLO = [mo["mhi0"], mo["mhi1"]], [mo["mlo0"], mo["mlo1"]]
        IOTA = cst[:, C_IOTA:C_IOTA + P]

        def moe_split(m, e, s):
            b = base[f"moe{m}"]
            return (b + MOE_PIECES * e + s, 0) if type(e) is int else (b + s, e)

        def moe_pe(pe, m, n):
            hT_ready(pe, n)
            pe.wait_ge(m_wl, m + 1)
            for k in range(KC):
                last = split3(pe, PS[0:NE, 4, 0:L], at((mo["wrh"], mo["wrl"]), slice(None), k, slice(None)),
                              at((hT_hi, hT_lo), slice(None), k, slice(None)), k == 0, k == KC - 1)
            last.then_inc(m_lt, 1)
            pe.wait_ge(m_lc, m + 1)
            for t in range(TT):
                last = pe.transpose(PS[:, 5, t * NE:(t + 1) * NE], mo["lgt"][:, t * P:(t + 1) * P], ident[0:NE, 0:NE])
            last.then_inc(m_lg, 1)
            pe.wait_ge(m_sel, m + 1)
            sel = mo["sel"]
            pe.matmul(PS[:, 3, 0:NE], ones, sel[:, 0, :], start=True, stop=False, skip_group_check=True)
            pe.matmul(PS[:, 3, 0:NE], ones, sel[:, 1, :], start=False, stop=True, skip_group_check=True)
            pe.matmul(PS[:, 5, 0:NE], lower, sel[:, 0, :], start=True, stop=True, skip_group_check=True)
            pe.matmul(PS[:, 5, NE:2 * NE], ones, sel[:, 0, :], start=True, stop=False, skip_group_check=True)
            pe.matmul(PS[:, 5, NE:2 * NE], lower, sel[:, 1, :], start=False, stop=True, skip_group_check=True)\
                .then_inc(m_rk, 1)

            def gather(e):
                g = NE * m + e
                pe.wait_ge(ex.pick, g + 1)
                if type(e) is int and e == 0:
                    pe.wait_ge(m_hl, TT * (m + 1))
                for half in range(2):
                    for t in range(TT):
                        for i, hx in enumerate((mo["hh"], mo["hl"])):
                            last = pe.matmul(PS[:, 6 + half, :], mo["pick"][:, t, :],
                                             hx[:, t, half * 512:half * 512 + 512],
                                             start=(t == 0 and i == 0), stop=(t == TT - 1 and i == 1),
                                             skip_group_check=True)
                last.then_inc(ex.gr, 1)

            def turn_tokens(e):
                g = NE * m + e
                pe.wait_ge(ex.copied, g + 1)
                for k in range(KC):
                    last = pe.transpose(PS[:, 6 + k // 4, (k % 4) * P:(k % 4 + 1) * P],
                                        mo["gt"][:, k * P:(k + 1) * P], ident)
                    if k % 4 == 3:
                        last.then_inc(ex.g, 1)

            def scatter(e):
                g = NE * m + e
                pe.wait_ge(ex.ylo, g + 1)
                for q, bank in enumerate((1, 6, 7, 4)):
                    t, half = q // 2, q % 2
                    c = slice(half * 512, half * 512 + 512)
                    pe.matmul(PS[:, bank, :], mo["put"][:, t, :], mo["ylo"][:, c], start=True, stop=False,
                              skip_group_check=True)
                    pe.matmul(PS[:, bank, :], mo["put"][:, t, :], mo["yhi"][:, c], start=False, stop=True,
                              skip_group_check=True).then_inc(ex.sc, 1)

            def expert(e, first, last_e):
                g = NE * m + e

                def gate_or_up(kind, j):
                    p, de = moe_split(m, e, NX[kind, j])
                    w = GU_E[j][1]
                    piece_ready(pe, p, de)
                    wp = wpiece(p, KC, w)
                    for k in range(KC):
                        last = split3(pe, PS[:, 0 if kind == "g" else 2, 0:w],
                                      at((hT_hi, hT_lo), slice(None), k, slice(0, P)),
                                      at(wp, slice(None), k, slice(None)), k == 0, k == KC - 1)
                    last.then_inc(w_used, 1)

                def turn(j):
                    pe.wait_ge(ex.mul, JE * g + j + 1)
                    if j >= 1:
                        pe.wait_ge(ex.alo, JE * g + j)
                    for c in range(GU_E[j][1] // P):
                        last = pe.transpose(PS[:, 3, c * P:(c + 1) * P], mo["mact"][:, c * P:(c + 1) * P], ident)
                    last.then_inc(ex.tp, 1)

                def down(j):
                    p, de = moe_split(m, e, NX["d", j])
                    kc = GU_E[j][1] // P
                    piece_ready(pe, p, de)
                    pe.wait_ge(ex.alo, JE * g + j + 1)
                    if j == 0:
                        pe.wait_ge(ex.put, g + 1)
                        if not first:
                            pe.wait_ge(ex.xa, 4 * g)
                    wp = wpiece(p, kc, D)
                    for half in range(2):
                        for c in range(kc):
                            s = slice(c * P, (c + 1) * P)
                            last = split3(pe, PS[:, 4 + half, :], (MHI[j % 2][:, s], MLO[j % 2][:, s]),
                                          at(wp, slice(None), c, slice(half * 512, half * 512 + 512)),
                                          j == 0 and c == 0, j == JE - 1 and c == kc - 1)
                    last.then_inc(w_used, 1)

                pe.wait_ge(ex.glo, 2 * (g + 1))
                gate_or_up("g", 0)
                gate_or_up("u", 0)
                if not first:
                    scatter(e - 1)
                for t in range(TT):
                    last = pe.transpose(PS[:, 5, t * P:(t + 1) * P], mo["pick"][:, t, :].bitcast(F32), ident)
                last.then_inc(ex.pt, 1)
                for j in range(1, JE):
                    if j == JE - 1 and not last_e:
                        gather(e + 1)
                    pe.wait_ge(ex.silu, JE * g + j)
                    gate_or_up("g", j)
                    if j == JE - 1 and not last_e:
                        turn_tokens(e + 1)
                    turn(j - 1)
                    if j >= 2:
                        down(j - 2)
                    gate_or_up("u", j)
                down(JE - 2)
                turn(JE - 1)
                down(JE - 1)

            gather(0)
            turn_tokens(0)
            expert(0, True, False)
            with pe.Fori(1, NE - 1) as e:
                expert(e, False, False)
            expert(NE - 1, False, True)
            scatter(NE - 1)
            rest_pe(pe, m)

        def moe_act(act, m, n):
            act.wait_ge(m_wr, 32 * (m + 1))
            act.activation(mo["wrh"][:], mo["wr"][:], ACT.Copy).then_inc(m_wh, 1)
            for t in range(TT):
                act.activation(mo["hh"][:, t, :], h[:, t, :], ACT.Copy).then_inc(m_hh, 1)
            act.wait_ge(m_gd, m + 1)
            act.activation(mo["gw"][:, :, 1:2], mo["gw"][:, :, 0:1], ACT.Exp).then_inc(m_ge, 1)

            def gathered(e):
                act.wait_ge(ex.gr, NE * m + e + 1)
                act.activation(mo["gt"][:], psf[:, 3072:4096], ACT.Copy).then_inc(ex.copied, 1)

            def ghi(e):
                g = NE * m + e
                for i in range(2):
                    act.wait_ge(ex.g, 2 * g + i + 1)
                    act.activation(hT_hi[:, 4 * i:4 * i + 4, 0:P], PS[:, 6 + i, :].rearrange("p (k s) -> p k s", k=4),
                                   ACT.Copy).then_inc(ex.ghi, 1)

            def expert(e, last_e):
                g = NE * m + e

                def sp_(kind, j):
                    p, de = moe_split(m, e, NX[kind, j])
                    split_hi(act, p + SPL, de)

                def used(kind, j):
                    p, de = moe_split(m, e, NX[kind, j])
                    act.wait_ge(w_used, p + 1 + MOE_PIECES * de)

                for j in range(JE + 1):
                    if j < JE:
                        w = GU_E[j][1]
                        if j == JE - 1 and not last_e:
                            gathered(e + 1)
                        used("g", j)
                        if j >= 1:
                            act.wait_ge(ex.mul, JE * g + j)
                        act.activation(mo["msg"][:, 0:w], PS[:, 0, 0:w], ACT.Silu).then_inc(ex.silu, 1)
                        sp_("g", j)
                    if j == 0:
                        sp_("u", 0)
                        act.wait_ge(ex.pt, g + 1)
                        act.activation(mo["put"][:].rearrange("p t s -> p (t s)"), PS[:, 5, 0:L], ACT.Copy)\
                            .then_inc(ex.put, 1)
                        continue
                    wm = GU_E[j - 1][1]
                    act.wait_ge(ex.tp, JE * g + j)
                    act.activation(MHI[(j - 1) % 2][:, 0:wm], PS[:, 3, 0:wm], ACT.Copy).then_inc(ex.ahi, 1)
                    if j < JE:
                        if j >= 2:
                            sp_("d", j - 2)
                        if j == JE - 1 and not last_e:
                            used("u", j)
                            ghi(e + 1)
                        sp_("u", j)
                    else:
                        sp_("d", JE - 2)
                used("d", JE - 1)
                act.activation(mo["yhi"][:], psf[:, 2048:3072], ACT.Copy).then_inc(ex.yhi, 1)
                if not last_e:
                    sp_("d", JE - 1)

            gathered(0)
            ghi(0)
            expert(0, False)
            with act.Fori(1, NE - 1) as e:
                expert(e, False)
            expert(NE - 1, True)
            rest_act(act, m)

        def moe_dve(dve, m, n):
            mk = [CHAIN_M[0]]

            def link(ins):
                mk[0] += 1
                ins.then_inc(chain_m, 1)
                dve.wait_ge(chain_m, mk[0])

            dve.wait_ge(m_wh, m + 1)
            dve.tensor_tensor(mo["wrl"][:], mo["wr"][:], mo["wrh"][:].bitcast(F32), ALU.subtract)\
                .then_inc(m_wl, 1)
            for t in range(TT):
                dve.wait_ge(m_hh, TT * m + t + 1)
                dve.tensor_tensor(mo["hl"][:, t, :], h[:, t, :], mo["hh"][:, t, :].bitcast(F32), ALU.subtract)\
                    .then_inc(m_hl, 1)
            lg, top, topi, topf, oh, sel, gw, route = (mo[k] for k in ("lg", "top", "topi", "topf", "oh", "sel", "gw",
                                                                       "route"))
            dve.wait_ge(m_lt, m + 1)
            dve.tensor_copy(mo["lgt"][:], PS[0:NE, 4, 0:L]).then_inc(m_lc, 1)
            dve.wait_ge(m_lg, m + 1)
            link(dve.tensor_tensor(lg[:], PS[:, 5, 0:TT * NE].rearrange("p (t e) -> p t e", t=TT),
                                   mo["rb"][:].rearrange("p (a e) -> p a e", a=1).to_broadcast([P, TT, NE]), ALU.add))
            dve.max(top[:, 0, :], lg[:, 0, :])
            link(dve.max(top[:, 1, :], lg[:, 1, :]))
            dve.tensor_tensor(gw[:, :, 0:1], top[:, :, 1:2], top[:, :, 0:1], ALU.subtract).then_inc(m_gd, 1)
            dve.max_index(topi[:, 0, :], top[:, 0, :], lg[:, 0, :])
            link(dve.max_index(topi[:, 1, :], top[:, 1, :], lg[:, 1, :]))
            link(dve.tensor_copy(topf[:], topi[:]))
            for t in range(TT):
                for j in range(2):
                    i = dve.tensor_scalar(oh[:, t, j, :], cst[:, C_IOTA:C_IOTA + NE], topf[:, t, j:j + 1], None,
                                          ALU.is_equal)
            link(i)
            dve.tensor_tensor(sel[:], oh[:, :, 0, :], oh[:, :, 1, :], ALU.add).then_inc(m_sel, 1)
            dve.wait_ge(m_ge, m + 1)
            link(dve.tensor_scalar(gw[:, :, 2:3], gw[:, :, 1:2], 1.0, None, ALU.add))
            link(dve.reciprocal(gw[:, :, 2:3], gw[:, :, 2:3]))
            link(dve.tensor_tensor(gw[:, :, 3:4], gw[:, :, 1:2], gw[:, :, 2:3], ALU.mult))
            for t in range(TT):
                dve.tensor_scalar(oh[:, t, 0, :], oh[:, t, 0, :], gw[:, t, 2:3], None, ALU.mult)
                i = dve.tensor_scalar(oh[:, t, 1, :], oh[:, t, 1, :], gw[:, t, 3:4], None, ALU.mult)
            dve.wait_ge(m_sel, m + 1)
            link(i)
            dve.wait_ge(m_rk, m + 1)
            for t in range(TT):
                dve.tensor_copy(route[:, :, 0, t], PS[:, 5, t * NE:(t + 1) * NE])
                dve.tensor_copy(route[:, :, 1, t], sel[:, t, :])
                i = dve.tensor_tensor(route[:, :, 2, t], oh[:, t, 0, :], oh[:, t, 1, :], ALU.add)
            link(i)
            link(dve.tensor_reduce(mo["cmx"][:], PS[:, 3, 0:NE], AX.X, ALU.max))
            CHAIN_M[0] = mk[0]
            dve.tensor_copy(most[:, m:m + 1], mo["cmx"][:]).then_inc(m_ovf, 1)

            def pick(e):
                g = NE * m + e
                src = route[:, e, 0:2, :] if type(e) is int else \
                    route[:, bass.ds(e, 1), 0:2, :].rearrange("p a b c -> p (a b) c")
                dve.tensor_copy(mo["cur"][:], src).then_inc(ex.cur, 1)
                dve.wait_ge(ex.cur, g + 1)
                for t in range(TT):
                    i = dve.tensor_scalar(mo["pick"][:, t, :], IOTA, mo["cur"][:, 0, t:t + 1], mo["cur"][:, 1, t:t + 1],
                                          ALU.is_equal, ALU.mult)
                i.then_inc(ex.pick, 1)

            def xadd(e):
                g = NE * m + e
                src = route[:, e, 2, :] if type(e) is int else \
                    route[:, bass.ds(e, 1), 2, :].rearrange("p a c -> p (a c)")
                dve.tensor_copy(mo["curg"][:], src).then_inc(ex.cug, 1)
                dve.wait_ge(ex.cug, g + 1)
                for q, bank in enumerate((1, 6, 7, 4)):
                    t, half = q // 2, q % 2
                    v = x[:, t, half * 512:half * 512 + 512]
                    dve.wait_ge(ex.sc, 4 * g + q + 1)
                    dve.scalar_tensor_tensor(out=v, in0=PS[:, bank, :], scalar=mo["curg"][:, t:t + 1], in1=v,
                                             op0=ALU.mult, op1=ALU.add).then_inc(ex.xa, 1)

            def glo(e):
                g = NE * m + e
                for i in range(2):
                    dve.wait_ge(ex.ghi, 2 * g + i + 1)
                    dve.tensor_tensor(hT_lo[:, 4 * i:4 * i + 4, 0:P], PS[:, 6 + i, :].rearrange("p (k s) -> p k s", k=4),
                                      hT_hi[:, 4 * i:4 * i + 4, 0:P].bitcast(F32), ALU.subtract).then_inc(ex.glo, 1)

            def expert(e, first, last_e):
                g = NE * m + e

                def sp_(kind, j):
                    p, de = moe_split(m, e, NX[kind, j])
                    split_lo(dve, p + SPL, de)

                def alo(j):
                    w = GU_E[j][1]
                    dve.wait_ge(ex.ahi, JE * g + j + 1)
                    dve.tensor_tensor(MLO[j % 2][:, 0:w], PS[:, 3, 0:w], MHI[j % 2][:, 0:w].bitcast(F32),
                                      ALU.subtract).then_inc(ex.alo, 1)

                for j in range(JE):
                    sp_("g", j)
                    if j >= 1:
                        alo(j - 1)
                    if j >= 2:
                        sp_("d", j - 2)
                    w = GU_E[j][1]
                    p, de = moe_split(m, e, NX["u", j])
                    dve.wait_ge(w_used, p + 1 + MOE_PIECES * de)
                    dve.wait_ge(ex.silu, JE * g + j + 1)
                    dve.tensor_tensor(mo["mact"][:, 0:w], PS[:, 2, 0:w], mo["msg"][:, 0:w], ALU.mult)\
                        .then_inc(ex.mul, 1)
                    if j == JE - 1 and not last_e:
                        glo(e + 1)
                    if j == JE - 1:
                        alo(j)
                    sp_("u", j)
                    if j == 0 and not first:
                        xadd(e - 1)
                    if j == 1 and not last_e:
                        dve.wait_ge(ex.pt, g + 1)
                        pick(e + 1)
                if not last_e:
                    sp_("d", JE - 2)
                dve.wait_ge(ex.yhi, g + 1)
                dve.tensor_tensor(mo["ylo"][:], psf[:, 2048:3072], mo["yhi"][:].bitcast(F32), ALU.subtract)\
                    .then_inc(ex.ylo, 1)
                if not last_e:
                    sp_("d", JE - 1)

            pick(0)
            for p0 in held_back(n, 2):
                split_lo(dve, p0)
            glo(0)
            expert(0, True, False)
            with dve.Fori(1, NE - 1) as e:
                expert(e, False, False)
            expert(NE - 1, False, True)
            xadd(NE - 1)
            dve.wait_ge(ex.xa, 4 * NE * (m + 1))
            rest_dve(dve, m)
            for t in range(TT):
                dve.sem_inc(x_up, 1)

        def moe_pool(pool, m, n):
            for t in range(TT):
                x_ready(pool, n, t)
            pool.dma_start(mo["wr"][:], w_router[m].rearrange("(k p) e -> p k e", p=P)).then_inc(m_wr, 16)
            pool.dma_start(mo["rb"][:], b_router[m].rearrange("(a e) -> a e", a=1).to_broadcast([P, NE]))\
                .then_inc(m_wr, 16)

        HB = FE // P

        class RestSems:
            def __init__(self, m):
                self.cur = sem(f"rest{m}_cur")
                self.pick = sem(f"rest{m}_pick")
                self.gath = sem(f"rest{m}_gath")
                self.gT = sem(f"rest{m}_gT")
                self.w = sem(f"rest{m}_w")
                self.gu = sem(f"rest{m}_gu")
                self.silu = sem(f"rest{m}_silu")
                self.act = sem(f"rest{m}_act")
                self.down = sem(f"rest{m}_down")
                self.y = sem(f"rest{m}_y")
                self.sc = sem(f"rest{m}_sc")
                self.xa = sem(f"rest{m}_xa")

        rest = [RestSems(m) for m in range(2)]
        SCB = (1, 3, 6, 7)

        def tokens_left(eng, m):
            eng.wait_ge(m_ovf, m + 1)
            return eng.value_load(most[0:1, m:m + 1], min_val=0, max_val=L) > CAP

        def rest_pe(pe, m):
            r = rest[m]
            with pe.If(tokens_left(pe, m)):
                pe.wait_ge(ex.xa, 4 * NE * (m + 1))
                with pe.Fori(0, NE) as e:
                    pe.wait_ge(r.pick, e + 1)
                    for k in range(KC):
                        for t in range(TT):
                            pe.matmul(PS[:, 6 + k // 4, (k % 4) * P:(k % 4 + 1) * P], h[:, t, k * P:(k + 1) * P],
                                      ov["opick"][:, t, :], start=(t == 0), stop=(t == TT - 1),
                                      skip_group_check=True)
                    for t in range(TT):
                        last = pe.transpose(PS[:, 5, t * P:(t + 1) * P], ov["opick"][:, t, :], ident)
                    last.then_inc(r.gath, 1)
                    with pe.Fori(0, HB) as j:
                        i = HB * e + j
                        pe.wait_ge(r.gT, e + 1)
                        pe.wait_ge(r.w, 48 * i + 48)
                        for bank, w in ((0, ov["owg"]), (2, ov["owu"])):
                            for k in range(KC):
                                last = pe.matmul(PS[:, bank, 0:P], w[:, k, :], ov["oT"][:, k, :], start=(k == 0),
                                                 stop=(k == KC - 1), skip_group_check=True)
                        last.then_inc(r.gu, 1)
                        pe.wait_ge(r.act, i + 1)
                        for half in range(2):
                            last = pe.matmul(PS[:, 4 + half, :], ov["oact"][:], ov["owd"][:, half * 512:half * 512 + 512],
                                             start=True, stop=True, skip_group_check=True)
                        last.then_inc(r.down, 1)
                        pe.wait_ge(r.y, i + 2 + e)
                    for q, bank in enumerate(SCB):
                        last = pe.matmul(PS[:, bank, :], ov["oput"][:, q // 2, :], ov["oy"][:, (q % 2) * 512:(q % 2) * 512 + 512],
                                         start=True, stop=True, skip_group_check=True)
                    last.then_inc(r.sc, 1)
                    pe.wait_ge(r.xa, e + 1)

        def rest_act(act, m):
            r = rest[m]
            with act.If(tokens_left(act, m)):
                with act.Fori(0, NE * HB) as i:
                    act.wait_ge(r.gu, i + 1)
                    act.activation(ov["osilu"][:], PS[:, 0, 0:P], ACT.Silu).then_inc(r.silu, 1)

        def rest_dve(dve, m):
            r = rest[m]
            route = mo["route"]
            with dve.If(tokens_left(dve, m)):
                with dve.Fori(0, NE) as e:
                    dve.tensor_copy(mo["cur"][:], route[:, bass.ds(e, 1), 0:2, :].rearrange("p a b c -> p (a b) c"))
                    dve.tensor_copy(mo["curg"][:], route[:, bass.ds(e, 1), 2, :].rearrange("p a c -> p (a c)"))\
                        .then_inc(r.cur, 1)
                    dve.wait_ge(r.cur, e + 1)
                    for t in range(TT):
                        last = dve.tensor_scalar(ov["opick"][:, t, :], cst[:, C_IOTA + P:C_IOTA + 2 * P],
                                                 mo["cur"][:, 0, t:t + 1], mo["cur"][:, 1, t:t + 1],
                                                 ALU.is_equal, ALU.mult)
                    last.then_inc(r.pick, 1)
                    dve.memset(ov["oy"][:], 0.0).then_inc(r.y, 1)
                    dve.wait_ge(r.gath, e + 1)
                    dve.tensor_copy(ov["oT"][:].rearrange("p k s -> p (k s)"), psf[:, 3072:4096])
                    dve.tensor_copy(ov["oput"][:].rearrange("p t s -> p (t s)"), PS[:, 5, 0:L]).then_inc(r.gT, 1)
                    with dve.Fori(0, HB) as j:
                        i = HB * e + j
                        dve.wait_ge(r.silu, i + 1)
                        dve.tensor_tensor(ov["oact"][:], PS[:, 2, 0:P], ov["osilu"][:], ALU.mult).then_inc(r.act, 1)
                        dve.wait_ge(r.down, i + 1)
                        dve.wait_ge(r.y, i + 1 + e)
                        dve.tensor_tensor(ov["oy"][:], psf[:, 2048:3072], ov["oy"][:], ALU.add).then_inc(r.y, 1)
                    dve.wait_ge(r.sc, e + 1)
                    for q, bank in enumerate(SCB):
                        v = x[:, q // 2, (q % 2) * 512:(q % 2) * 512 + 512]
                        last = dve.scalar_tensor_tensor(out=v, in0=PS[:, bank, :], scalar=mo["curg"][:, q // 2:q // 2 + 1],
                                                        in1=v, op0=ALU.mult, op1=ALU.add)
                    last.then_inc(r.xa, 1)
                    dve.wait_ge(r.xa, e + 1)

        def rest_pool(pool, m):
            r = rest[m]
            with pool.If(tokens_left(pool, m)):
                pool.wait_ge(ex.xa, 4 * NE * (m + 1))
                with pool.Fori(0, NE) as e:
                    with pool.Fori(0, HB) as j:
                        gu = moe_w_gate_up[m, bass.ds(e, 1), :, :].rearrange("a (k p) n -> p (a k) n", p=P)
                        down = moe_w_down[m, bass.ds(e, 1), bass.ds(j * P, P), :].rearrange("a r n -> (a r) n")
                        pool.wait_ge(r.y, HB * e + j + 1 + e)
                        pool.dma_start(ov["owg"][:], gu[:, :, bass.ds(j * P, P)]).then_inc(r.w, 16)
                        pool.dma_start(ov["owu"][:], gu[:, :, bass.ds(j * P + FE, P)]).then_inc(r.w, 16)
                        pool.dma_start(ov["owd"][:], down).then_inc(r.w, 16)

        l_mg, l_sq, l_ms, l_rs, l_cn, l_tp, l_hi, l_lo, l_kr = (
            sem("l_mg"), sem("l_sq"), sem("l_ms"), sem("l_rs"), sem("l_cn"), sem("l_tp"), sem("l_hi"), sem("l_lo"),
            sem("l_kr"))
        l_qa, l_qd, l_rope, l_va, l_vd, l_qt, l_qe, l_kn, l_ke = (
            sem("l_qa"), sem("l_qd"), sem("l_rope"), sem("l_va"), sem("l_vd"), sem("l_qt"), sem("l_qe"),
            sem("l_kn"), sem("l_ke"))
        l_s, l_m, l_p, l_t, l_e, l_v, l_o, l_ot, l_oh, l_ol = (
            sem("l_s"), sem("l_m"), sem("l_p"), sem("l_t"), sem("l_e"), sem("l_v"), sem("l_o"), sem("l_ot"),
            sem("l_oh"), sem("l_ol"))
        CN = QR + KVR
        HG = HEADS // 2
        cn, mg, rt = ml["cn"], ml["mg"], ml["rt"]
        kTm, qTm, vm, qt = ml["kTm"], ml["qTm"], ml["vm"], ml["qt"]
        cosv = cst[:, C_COS:C_COS + 32].rearrange("p (t f) -> p t f", t=TT)
        sinv = cst[:, C_SIN:C_SIN + 32].rearrange("p (t f) -> p t f", t=TT)

        def mla_pool(pool):
            for t in range(TT):
                x_ready(pool, 4, t)
            pool.dma_start(mg[:, 0:QR], mla_q_norm[0].rearrange("(a d) -> a d", a=1).to_broadcast([P, QR]))\
                .then_inc(l_mg, 16)
            pool.dma_start(mg[:, QR:CN], mla_kv_norm[0].rearrange("(a d) -> a d", a=1).to_broadcast([P, KVR]))\
                .then_inc(l_mg, 16)

        def mla_pool2(pool):
            pool.wait_ge(l_ms, 2)
            pool.tensor_tensor(ml["st"][:, 8:12], ml["st"][:, 4:8], cst[:, C_POW:C_POW + 1].to_broadcast([P, 4]), ALU.pow)\
                .then_inc(l_rs, 1)

        def mla_pe(pe):
            b0 = base["mla"]
            hT_ready(pe, 4)
            for q, w in enumerate((QR, KVR + ROPE)):
                piece_ready(pe, b0 + q)
                wp = wpiece(b0 + q, KC, w)
                for t in range(TT):
                    for k in range(KC):
                        last = split3(pe, PS[:, 2 * q + t, 0:w],
                                      at((hT_hi, hT_lo), slice(None), k, slice(t * P, (t + 1) * P)),
                                      at(wp, slice(None), k, slice(None)), k == 0, k == KC - 1)
                last.then_inc(w_used, 1)
            pe.wait_ge(l_cn, 1)
            for t in range(TT):
                for c in range(CN // P):
                    o = 2048 + c * L + t * P
                    pe.transpose(psf[:, o:o + P], cn[:, t, c * P:(c + 1) * P], ident)
                last = pe.transpose(PS[0:QH, 7, t * P:(t + 1) * P], cn[:, t, CN + ROPE - QH:CN + ROPE], ident)
            last.then_inc(l_tp, 1)
            pe.wait_ge(l_lo, 1)
            pe.wait_ge(l_kr, 2)
            for i in range(2):
                p = b0 + 2 + 2 * i
                piece_ready(pe, p)
                wp = wpiece(p, QR // P, HG * QH)
                if i == 1:
                    pe.wait_ge(l_va, 1)
                    pe.wait_ge(l_vd, 1)
                for t in range(TT):
                    for half in range(2):
                        for k in range(QR // P):
                            last = split3(pe, PS[:, 2 * t + half, 0:384],
                                          at((hT_hi, hT_lo), slice(None), k, slice(t * P, (t + 1) * P)),
                                          at(wp, slice(None), k, slice(half * 384, half * 384 + 384)),
                                          k == 0, k == QR // P - 1)
                last.then_inc(w_used, 1)
                p = b0 + 3 + 2 * i
                piece_ready(pe, p)
                wp = wpiece(p, KVR // P, HG * P)
                if i == 1:
                    pe.wait_ge(l_qe, 4)
                for j in range(HG):
                    for k in range(KVR // P):
                        last = split3(pe, PS[:, 4 + j // 2, (j % 2) * L:(j % 2 + 1) * L],
                                      at(wp, slice(None), k, slice(j * P, (j + 1) * P)),
                                      at((hT_hi, hT_lo), slice(None), QR // P + k, slice(None)), k == 0,
                                      k == KVR // P - 1)
                last.then_inc(l_kn, 1)
                pe.wait_ge(l_qa, i + 1)
                pe.wait_ge(l_qd, i + 1)
                for t in range(TT):
                    for k in range(KVR // P):
                        v = tuple(q.rearrange("p k (h c) -> p k h c", c=P)[:, k, :, NOPE:P] for q in wp)
                        last = split3(pe, PS[:, t, :], at((hT_hi, hT_lo), slice(None), QR // P + k, slice(t * P, (t + 1) * P)),
                                      v, k == 0, k == KVR // P - 1)
                last.then_inc(w_used, 1)
                pe.wait_ge(l_rope, i + 1)
                pe.wait_ge(l_ke, 4 * (i + 1))
                for j in range(HG):
                    for t in range(TT):
                        last = pe.transpose(PS[0:QH, 4 + j // 2, (j % 2) * L + t * P:(j % 2) * L + (t + 1) * P],
                                            qt[:, t, j * QH:(j + 1) * QH], ident)
                    if j % 2:
                        last.then_inc(l_qt, 1)

            def scores(i):
                if i == 0:
                    pe.wait_ge(l_qe, 8)
                    pe.wait_ge(l_va, 2)
                    pe.wait_ge(l_vd, 2)
                if i >= 4:
                    pe.wait_ge(l_p, i - 3)
                s = PS[:, i % 4, :]
                pe.matmul(s[:, 0:P], qTm[:, i, 0:P], kTm[:, i, 0:P], start=True, stop=False, skip_group_check=True)
                pe.matmul(s[:, P:P + L], qTm[:, i, P:L], kTm[:, i, 0:L], start=False, stop=False,
                          skip_group_check=True)
                pe.matmul(s[:, 0:P], ident, causal, start=False, stop=True, skip_group_check=True)
                pe.matmul(s[:, L:L + P], ident, causal, start=False, stop=True, skip_group_check=True)\
                    .then_inc(l_s, 1)

            def turn(i):
                pe.wait_ge(l_p, i + 1)
                if i >= 2:
                    pe.wait_ge(l_e, i - 1)
                for c in range(3):
                    last = pe.transpose(PS[:, 4 + i % 2, c * P:(c + 1) * P], ml[f"pb{i % 4}"][:, c * P:(c + 1) * P], ident)
                last.then_inc(l_t, 1)

            def values(i):
                pe.wait_ge(l_e, i + 1)
                if i == HG:
                    pe.wait_ge(l_ol, 1)
                w = ml[f"pt{i % 2}"]
                c, o = slice(i * MV, (i + 1) * MV), slice((i % HG) * MV, (i % HG + 1) * MV)
                pe.matmul(PS[:, 6, o], w[:, 0:P], vm[:, 0, c], start=True, stop=True, skip_group_check=True)
                pe.matmul(PS[:, 7, o], w[:, P:2 * P], vm[:, 0, c], start=True, stop=False, skip_group_check=True)
                pe.matmul(PS[:, 7, o], w[:, 2 * P:3 * P], vm[:, 1, c], start=False, stop=True,
                          skip_group_check=True).then_inc(l_v, 1)
                if i % HG == HG - 1:
                    g = i // HG
                    pe.wait_ge(l_o, g + 1)
                    for c in range(4):
                        for t in range(TT):
                            last = pe.transpose(psf[:, 3072 + c * L + t * P:3072 + c * L + (t + 1) * P],
                                                ml["ot"][:, t, c * P:(c + 1) * P], ident)
                    last.then_inc(l_ot, 1)

            for i in range(HEADS + 3):
                if i < HEADS:
                    scores(i)
                if 2 <= i < HEADS + 2:
                    turn(i - 2)
                if i >= 3:
                    values(i - 3)
            pe.wait_ge(l_ol, 2)
            proj_pe(pe, b0 + 6)

        def mla_act(act):
            b0 = base["mla"]
            for q, w in enumerate((QR, KVR)):
                act.wait_ge(w_used, b0 + q + 1)
                for t in range(TT):
                    act.activation(cn[:, t, q * QR:q * QR + w], PS[:, 2 * q + t, 0:w], ACT.Square,
                                   accum_out=ml["st"][:, 2 * q + t:2 * q + t + 1]).then_inc(l_sq, 1)
                split_hi(act, b0 + q + SPL)
            act.wait_ge(l_tp, 1)
            act.activation(hT_hi[:, 0:CN // P, :].rearrange("p k l -> p (k l)"), psf[:, 2048:2048 + CN // P * L], ACT.Copy)\
                .then_inc(l_hi, 1)
            kr = PS[NOPE:QH, 7, 0:L].rearrange("p (a l) -> p a l", a=1).to_broadcast([ROPE, HG, L])
            act.activation(kTm[NOPE:QH, 0:HG, :], kr, ACT.Copy).then_inc(l_kr, 1)
            for i in range(2):
                act.wait_ge(w_used, b0 + 3 + 2 * i)
                if i == 1:
                    act.wait_ge(l_qt, 4)
                act.activation(qt[:, 0, :].rearrange("p (a n) -> p a n", a=2), PS[:, 0:2, 0:384], ACT.Copy)\
                    .then_inc(l_qa, 1)
                split_hi(act, b0 + 2 + 2 * i + SPL)
                act.wait_ge(l_kn, i + 1)
                for j in range(0, 4, 2):
                    act.activation(kTm[0:NOPE, HG * i + 2 * j:HG * i + 2 * j + 2, :],
                                   PS[0:NOPE, 4 + j, :].rearrange("p (a l) -> p a l", a=2), ACT.Copy).then_inc(l_ke, 1)
                act.wait_ge(w_used, b0 + 4 + 2 * i)
                act.activation(vm[:, 0, 512 * i:512 * i + 512], PS[:, 0, :], ACT.Copy).then_inc(l_va, 1)
                split_hi(act, b0 + 3 + 2 * i + SPL)
                for j in range(0, 4, 2):
                    act.wait_ge(l_qt, 4 * i + j + 1)
                    act.activation(qTm[:, HG * i + 2 * j:HG * i + 2 * j + 2, :],
                                   PS[0:QH, 4 + j, :].rearrange("p (a l) -> p a l", a=2), ACT.Copy).then_inc(l_qe, 1)
            for i in range(HEADS + 5):
                if i < HEADS:
                    act.wait_ge(l_m, i + 1)
                    if i >= 4:
                        act.wait_ge(l_t, i - 3)
                    pb = ml[f"pb{i % 4}"]
                    for t, (c, w) in enumerate(((0, P), (P, L))):
                        ins = act.activation(pb[:, c:c + w], PS[:, i % 4, c:c + w], ACT.Exp,
                                             bias=ml["nm"][:, i % 4, t:t + 1], scale=MLA_SCALE,
                                             accum_out=ml["sm"][:, i, t:t + 1])
                    ins.then_inc(l_p, 1)
                if i % HG == 2 and i > HG:
                    out_hi(act, i // HG - 1)
            proj_act(act, b0 + 6)

        def out_hi(act, g):
            act.wait_ge(l_ot, g + 1)
            act.activation(hT_hi[:, 4 * g:4 * g + 4, :].rearrange("p k l -> p (k l)"), psf[:, 3072:4096], ACT.Copy)\
                .then_inc(l_oh, 1)

        def mla_dve(dve):
            b0 = base["mla"]
            st = ml["st"]
            k = [CHAIN_M[0]]

            def link(ins):
                k[0] += 1
                ins.then_inc(chain_m, 1)
                dve.wait_ge(chain_m, k[0])

            for q, w in enumerate((QR, KVR)):
                dve.wait_ge(l_sq, 2 * q + 2)
                dve.tensor_scalar(st[:, 4 + 2 * q:6 + 2 * q], st[:, 2 * q:2 * q + 2], 1.0 / w, EPS, ALU.mult, ALU.add)\
                    .then_inc(l_ms, 1)
            r1, r2 = PS[:, 2:4, KVR:KVR + 16], PS[:, 2:4, KVR + 16:KVR + 32]
            tmp = [rt[:, q * 32:(q + 1) * 32].rearrange("p (t f) -> p t f", t=TT) for q in range(4)]
            for o, a, b in zip(tmp, (r1, r2, r1, r2), (cosv, sinv, sinv, cosv)):
                i = dve.tensor_tensor(o, a, b, ALU.mult)
            link(i)
            dve.tensor_tensor(cn[:, :, CN:CN + 16], tmp[0], tmp[1], ALU.subtract)
            dve.tensor_tensor(cn[:, :, CN + 16:CN + 32], tmp[2], tmp[3], ALU.add)
            dve.wait_ge(l_rs, 1)
            dve.wait_ge(l_mg, 32)
            for q, w in enumerate((QR, KVR)):
                for t in range(TT):
                    i = dve.scalar_tensor_tensor(out=cn[:, t, q * QR:q * QR + w], in0=PS[:, 2 * q + t, 0:w],
                                                 scalar=st[:, 8 + 2 * q + t:9 + 2 * q + t], in1=mg[:, q * QR:q * QR + w],
                                                 op0=ALU.mult, op1=ALU.mult)
            i.then_inc(l_cn, 1)
            split_lo(dve, b0 + SPL)
            split_lo(dve, b0 + 1 + SPL)
            dve.wait_ge(l_hi, 1)
            dve.tensor_tensor(hT_lo[:, 0:CN // P, :].rearrange("p k l -> p (k l)"), psf[:, 2048:2048 + CN // P * L],
                              hT_hi[:, 0:CN // P, :].rearrange("p k l -> p (k l)").bitcast(F32), ALU.subtract)\
                .then_inc(l_lo, 1)
            kr = PS[NOPE:QH, 7, 0:L].rearrange("p (a l) -> p a l", a=1).to_broadcast([ROPE, HG, L])
            dve.wait_ge(l_kr, 1)
            dve.tensor_copy(kTm[NOPE:QH, HG:HEADS, :], kr).then_inc(l_kr, 1)
            qv = qt[:].rearrange("p t (h c) -> p t h c", c=QH)
            rv = [rt[:, q * 256:(q + 1) * 256].rearrange("p (t h f) -> p t h f", t=TT, h=HG) for q in range(4)]
            cb = cosv.rearrange("p t (a f) -> p t a f", a=1).to_broadcast([P, TT, HG, 16])
            sbb = sinv.rearrange("p t (a f) -> p t a f", a=1).to_broadcast([P, TT, HG, 16])
            q1, q2 = qv[:, :, :, NOPE:NOPE + 16], qv[:, :, :, NOPE + 16:QH]
            for i in range(2):
                dve.wait_ge(w_used, b0 + 3 + 2 * i)
                if i == 1:
                    dve.wait_ge(l_qt, 4)
                dve.tensor_copy(qt[:, 1, :].rearrange("p (a n) -> p a n", a=2), PS[:, 2:4, 0:384]).then_inc(l_qd, 1)
                dve.wait_ge(l_qd, i + 1)
                dve.wait_ge(l_qa, i + 1)
                for o, a, b in zip(rv, (q1, q2, q1, q2), (cb, sbb, sbb, cb)):
                    j = dve.tensor_tensor(o, a, b, ALU.mult)
                link(j)
                dve.tensor_tensor(q1, rv[0], rv[1], ALU.subtract)
                dve.tensor_tensor(q2, rv[2], rv[3], ALU.add).then_inc(l_rope, 1)
                split_lo(dve, b0 + 2 + 2 * i + SPL)
                dve.wait_ge(l_kn, i + 1)
                for j in range(1, 4, 2):
                    dve.tensor_copy(kTm[0:NOPE, HG * i + 2 * j:HG * i + 2 * j + 2, :],
                                    PS[0:NOPE, 4 + j, :].rearrange("p (a l) -> p a l", a=2)).then_inc(l_ke, 1)
                dve.wait_ge(w_used, b0 + 4 + 2 * i)
                dve.tensor_copy(vm[:, 1, 512 * i:512 * i + 512], PS[:, 1, :]).then_inc(l_vd, 1)
                split_lo(dve, b0 + 3 + 2 * i + SPL)
                for j in range(1, 4, 2):
                    dve.wait_ge(l_qt, 4 * i + j + 1)
                    dve.tensor_copy(qTm[:, HG * i + 2 * j:HG * i + 2 * j + 2, :],
                                    PS[0:QH, 4 + j, :].rearrange("p (a l) -> p a l", a=2)).then_inc(l_qe, 1)

            def take(i):
                dve.wait_ge(l_t, i + 1)
                if i >= 2:
                    dve.wait_ge(l_v, i - 1)
                dve.tensor_copy(ml[f"pt{i % 2}"][:], PS[:, 4 + i % 2, 0:384]).then_inc(l_e, 1)

            def norm_out(g):
                dve.wait_ge(l_v, HG * (g + 1))
                link(dve.reciprocal(ml["ri"][:], ml["sm"][:, HG * g:HG * (g + 1), :].rearrange("p h t -> p t h")))
                for t in range(TT):
                    r = ml["ri"][:, t, :].rearrange("p (h a) -> p h a", a=1).to_broadcast([P, HG, MV])
                    j = dve.tensor_tensor(ml["ot"][:, t, :].rearrange("p (h c) -> p h c", h=HG),
                                          PS[:, 6 + t, :].rearrange("p (h c) -> p h c", h=HG), r, ALU.mult)
                j.then_inc(l_o, 1)

            def out_lo(g):
                dve.wait_ge(l_oh, g + 1)
                dve.tensor_tensor(hT_lo[:, 4 * g:4 * g + 4, :].rearrange("p k l -> p (k l)"), psf[:, 3072:4096],
                                  hT_hi[:, 4 * g:4 * g + 4, :].rearrange("p k l -> p (k l)").bitcast(F32),
                                  ALU.subtract).then_inc(l_ol, 1)

            for i in range(HEADS + 4):
                if i < HEADS:
                    dve.wait_ge(l_s, i + 1)
                    if i >= 4:
                        dve.wait_ge(l_p, i - 3)
                    s, mx = PS[:, i % 4, :], ml["mx"][:, i % 4, :]
                    dve.tensor_reduce(mx[:, 0:1], s[:, 0:P], AX.X, ALU.max)
                    link(dve.tensor_reduce(mx[:, 1:2], s[:, P:P + L], AX.X, ALU.max))
                    dve.tensor_scalar(ml["nm"][:, i % 4, :], mx, -MLA_SCALE, None, ALU.mult).then_inc(l_m, 1)
                if 2 <= i < HEADS + 2:
                    take(i - 2)
                if i % HG == 2 and i > HG:
                    norm_out(i // HG - 1)
                if i % HG == 3 and i > HG:
                    out_lo(i // HG - 1)
            CHAIN_M[0] = k[0]
            proj_dve(dve, b0 + 6)

        block = ctx.enter_context(nc.Block())

        @block.sync
        def _(sp):
            sp_program(sp)

        @block.scalar
        def _(act):
            norm_act(act, 0)
            for p0 in range(SPL):
                split_hi(act, p0)
            s5_setup_act(act)
            s5_setup_act2(act)
            sb_act(act, 0, 0)
            norm_act(act, 1)
            dense_act(act, 0, 1)
            norm_act(act, 2)
            s5_act(act)
            norm_act(act, 3)
            moe_act(act, 0, 3)
            norm_act(act, 4)
            mla_act(act)
            norm_act(act, 5)
            dense_act(act, 1, 5)
            norm_act(act, 6)
            sb_act(act, 1, 6)
            norm_act(act, 7)
            moe_act(act, 1, 7)
            norm_act(act, 8)

        @block.vector
        def _(dve):
            norm_dve(dve, 0)
            for p0 in range(SPL):
                split_lo(dve, p0)
            sb_dve(dve, 0, 0)
            norm_dve(dve, 1)
            dense_dve(dve, 0, 1)
            norm_dve(dve, 2)
            s5_dve(dve)
            norm_dve(dve, 3)
            moe_dve(dve, 0, 3)
            norm_dve(dve, 4)
            mla_dve(dve)
            norm_dve(dve, 5)
            dense_dve(dve, 1, 5)
            norm_dve(dve, 6)
            sb_dve(dve, 1, 6)
            norm_dve(dve, 7)
            moe_dve(dve, 1, 7)
            norm_dve(dve, 8)

        @block.gpsimd
        def _(pool):
            s5_setup_pool(pool)
            norm_pool(pool, 0)
            s5_setup_pool2(pool)
            sb_pool(pool, 0, 0)
            norm_pool(pool, 1)
            s5_tables_pool(pool)
            s5_mats_pool(pool)
            norm_pool(pool, 2)
            s5_pool(pool)
            moe_pool(pool, 0, 3)
            norm_pool(pool, 3)
            rest_pool(pool, 0)
            mla_pool(pool)
            norm_pool(pool, 4)
            mla_pool2(pool)
            norm_pool(pool, 5)
            norm_pool(pool, 6)
            sb_pool(pool, 1, 6)
            moe_pool(pool, 1, 7)
            norm_pool(pool, 7)
            rest_pool(pool, 1)
            norm_pool(pool, 8)

        @block.tensor
        def _(pe):
            norm_pe(pe, 0)
            sb_pe(pe, 0, 0)
            norm_pe(pe, 1)
            dense_pe(pe, 0, 1)
            s5_prep_pe(pe)
            norm_pe(pe, 2)
            s5_pe(pe)
            norm_pe(pe, 3)
            moe_pe(pe, 0, 3)
            norm_pe(pe, 4)
            mla_pe(pe)
            norm_pe(pe, 5)
            dense_pe(pe, 1, 5)
            norm_pe(pe, 6)
            sb_pe(pe, 1, 6)
            norm_pe(pe, 7)
            moe_pe(pe, 1, 7)


_INS = ["x", "norm_mix", "norm_ffn", "final_norm", "sb_w_qkv", "sb_w_o", "s5_lambda_re", "s5_lambda_im", "s5_log_dt",
        "s5_b_re", "s5_b_im", "s5_c_re", "s5_c_im", "s5_d", "s5_w_glu", "mla_w_in", "mla_q_norm", "mla_w_q_b",
        "mla_kv_norm", "mla_w_kv_b", "mla_w_o", "ffn_w_gate_up", "ffn_w_down", "moe_w_router", "moe_b_router",
        "moe_w_gate_up", "moe_w_down"]


def kernel(**inputs):
    import concourse.bacc as bacc
    from concourse.bass_utils import run_bass_kernel_spmd

    nc = bacc.Bacc("TRN2", target_bir_lowering=False, num_devices=1)
    arrays = {"in_consts": constants()}
    args = [nc.dram_tensor("in_consts", [P, C_END], F32, kind="ExternalInput").ap()]
    for name in _INS:
        a = np.ascontiguousarray(inputs[name])
        arrays[f"in_{name}"] = a
        args.append(nc.dram_tensor(f"in_{name}", a.shape, mybir.dt.from_np(a.dtype), kind="ExternalInput").ap())
    args.append(nc.dram_tensor("out_0", [1, L, D], F32, kind="ExternalOutput").ap())
    hybrid_trunk(nc, *args)
    r = run_bass_kernel_spmd(nc, [arrays], core_ids=[0])
    return r.results[0]["out_0"]
```
